# Optimizing a Trainium2 kernel written in Bass

```python
import numpy as np
import jax
import jax.numpy as jnp
from jax import lax
import math
import jax, jax.numpy as jnp

D_MODEL = 1024
BATCH = 1
SEQ = 1024
DEPTH = 2

HEAD_DIM = 64
N_MIXERS = 2
A_Q_HEADS = 16
A_KV_HEADS = 4
A_HALF_WINDOW = 128
B_GROUPS = ((128, 1), (512, 4), (2048, 16))
B_Q_HEADS = 8
B_KV_HEADS = 2
D_FF = -(-8 * D_MODEL // (3 * 256)) * 256
A_QKV = (A_Q_HEADS + 2 * A_KV_HEADS) * HEAD_DIM
B_QKV = len(B_GROUPS) * (B_Q_HEADS + 2 * B_KV_HEADS) * HEAD_DIM
A_OUT = A_Q_HEADS * HEAD_DIM
B_OUT = B_Q_HEADS * HEAD_DIM
N_A_LAYERS = (DEPTH + 1) // 2
N_B_LAYERS = DEPTH // 2
RMS_EPS = 1e-6
NEG = -1e30


def rmsnorm(x, g):
    xf = x.astype(jnp.float32)
    y = xf * lax.rsqrt(jnp.mean(xf * xf, axis=-1, keepdims=True) + RMS_EPS)
    return (y * g.astype(jnp.float32)).astype(x.dtype)

def alibi_slopes(n):
    return jnp.asarray(2.0 ** (-8.0 * np.arange(1, n + 1) / n), dtype=jnp.float32)

def banded_attention(q, k, v, half_window, slopes, dist_scale, sink=None):
    n, L, hkv, g, dh = q.shape
    blk = half_window
    nb = -(-L // blk)
    lp = nb * blk
    qb = jnp.pad(q, ((0, 0), (0, lp - L), (0, 0), (0, 0), (0, 0))).reshape(n, nb, blk, hkv, g, dh)
    pad_kv = ((0, 0), (blk, lp - L + blk), (0, 0), (0, 0))
    kb = jnp.pad(k, pad_kv).reshape(n, nb + 2, blk, hkv, dh)
    vb = jnp.pad(v, pad_kv).reshape(n, nb + 2, blk, hkv, dh)
    kw = jnp.concatenate([kb[:, :-2], kb[:, 1:-1], kb[:, 2:]], axis=2)
    vw = jnp.concatenate([vb[:, :-2], vb[:, 1:-1], vb[:, 2:]], axis=2)
    rel = jnp.arange(3 * blk)[None, :] - blk - jnp.arange(blk)[:, None]
    kpos = jnp.arange(nb)[:, None] * blk - blk + jnp.arange(3 * blk)[None, :]
    mask = (jnp.abs(rel) <= half_window)[None] & ((kpos >= 0) & (kpos < L))[:, None, :]
    dist = (dist_scale * jnp.abs(rel)).astype(jnp.float32)
    bias = -slopes.astype(jnp.float32)[:, :, None, None] * dist
    s = jnp.einsum('nbqhgd,nbkhd->nbhgqk', qb, kw,
                   preferred_element_type=jnp.float32) * (dh ** -0.5) + bias
    s = jnp.where(mask[None, :, None, None], s, NEG)
    m = s.max(axis=-1)
    if sink is not None:
        sk = sink.astype(jnp.float32)[:, :, None]
        m = jnp.maximum(m, sk)
    p = jnp.exp(s - m[..., None])
    l = p.sum(axis=-1)
    if sink is not None:
        l = l + jnp.exp(sk - m)
    o = jnp.einsum('nbhgqk,nbkhd->nbqhgd', p, vw.astype(jnp.float32))
    o = o / jnp.moveaxis(l, -1, 2)[..., None]
    lse = jnp.moveaxis(m + jnp.log(l), -1, 2)
    o = o.reshape(n, lp, hkv, g, dh)[:, :L].astype(q.dtype)
    lse = lse.reshape(n, lp, hkv, g)[:, :L]
    return o, lse

def to_strided(t, dil):
    b, s = t.shape[:2]
    rest = t.shape[2:]
    t = t.reshape(b, s // dil, dil, *rest)
    return jnp.moveaxis(t, 2, 1).reshape(b * dil, s // dil, *rest)

def from_strided(t, b, dil):
    l = t.shape[1]
    rest = t.shape[2:]
    t = t.reshape(b, dil, l, *rest)
    return jnp.moveaxis(t, 1, 2).reshape(b, l * dil, *rest)

def windowed_gqa(h, w_in, w_out, sink):
    b, s, _ = h.shape
    gq = A_Q_HEADS // A_KV_HEADS
    dq, dk = A_Q_HEADS * HEAD_DIM, A_KV_HEADS * HEAD_DIM
    qkv = h @ w_in
    q = qkv[..., :dq].reshape(b, s, A_KV_HEADS, gq, HEAD_DIM)
    k = qkv[..., dq:dq + dk].reshape(b, s, A_KV_HEADS, HEAD_DIM)
    v = qkv[..., dq + dk:].reshape(b, s, A_KV_HEADS, HEAD_DIM)
    slopes = alibi_slopes(A_Q_HEADS).reshape(A_KV_HEADS, gq)
    o, _ = banded_attention(q, k, v, A_HALF_WINDOW, slopes, 1, sink.reshape(A_KV_HEADS, gq))
    return o.reshape(b, s, A_OUT) @ w_out

def dilated_attention(h, w_in, w_out):
    b, s, _ = h.shape
    ng = len(B_GROUPS)
    gq = B_Q_HEADS // B_KV_HEADS
    dq, dk = ng * B_Q_HEADS * HEAD_DIM, ng * B_KV_HEADS * HEAD_DIM
    qkv = h @ w_in
    q = qkv[..., :dq].reshape(b, s, ng, B_KV_HEADS, gq, HEAD_DIM)
    k = qkv[..., dq:dq + dk].reshape(b, s, ng, B_KV_HEADS, HEAD_DIM)
    v = qkv[..., dq + dk:].reshape(b, s, ng, B_KV_HEADS, HEAD_DIM)
    slopes = alibi_slopes(ng * B_Q_HEADS).reshape(ng, B_KV_HEADS, gq)
    outs, lses = [], []
    for gi, (window, dil) in enumerate(B_GROUPS):
        half = window // (2 * dil)
        o, lse = banded_attention(to_strided(q[:, :, gi], dil), to_strided(k[:, :, gi], dil),
                                  to_strided(v[:, :, gi], dil), half, slopes[gi], dil)
        outs.append(from_strided(o, b, dil))
        lses.append(from_strided(lse, b, dil))
    alpha = jax.nn.softmax(jnp.stack(lses), axis=0)
    o = jnp.einsum('nbshg,nbshgd->bshgd', alpha,
                   jnp.stack(outs).astype(jnp.float32)).astype(h.dtype)
    return o.reshape(b, s, B_OUT) @ w_out

def swiglu(h, w_in, w_out):
    gu = h @ w_in
    gate, up = jnp.split(gu, 2, axis=-1)
    return (jax.nn.silu(gate) * up) @ w_out

def first_inputs(seed: int = 0) -> dict:
    key = jax.random.key(seed)
    ks = jax.random.split(key, 16)
    D = D_MODEL
    nrm = lambda k, shape, scale: jax.random.normal(k, shape, jnp.float32) * scale
    return {
        "x": nrm(ks[0], (BATCH, SEQ, D), 1.0),
        "c": nrm(ks[1], (BATCH, D), 1.0),
        "ada_w": nrm(ks[2], (DEPTH, D, 6 * D), 0.5 * D ** -0.5),
        "ada_b": nrm(ks[3], (DEPTH, 6 * D), 0.1),
        "norm_mix": 1.0 + nrm(ks[4], (DEPTH, D), 0.05),
        "norm_ffn": 1.0 + nrm(ks[5], (DEPTH, D), 0.05),
        "ffn_w_in": nrm(ks[6], (DEPTH, D, 2 * D_FF), D ** -0.5),
        "ffn_w_out": nrm(ks[7], (DEPTH, D_FF, D), D_FF ** -0.5),
        "a_w_in": nrm(ks[8], (N_A_LAYERS, D, A_QKV), D ** -0.5),
        "a_w_out": nrm(ks[9], (N_A_LAYERS, A_OUT, D), A_OUT ** -0.5),
        "a_sink": nrm(ks[10], (N_A_LAYERS, A_Q_HEADS), 0.5),
        "b_w_in": nrm(ks[11], (N_B_LAYERS, D, B_QKV), D ** -0.5),
        "b_w_out": nrm(ks[12], (N_B_LAYERS, B_OUT, D), B_OUT ** -0.5),
        "final_norm": 1.0 + nrm(ks[13], (D,), 0.05),
    }

def first_block(x, c, ada_w, ada_b, norm_mix, norm_ffn, ffn_w_in, ffn_w_out,
              a_w_in, a_w_out, a_sink, b_w_in, b_w_out, final_norm):
    cond = jax.nn.silu(c)
    for i in range(DEPTH):
        mod = (cond @ ada_w[i] + ada_b[i])[:, None, :]
        sh1, sc1, g1, sh2, sc2, g2 = jnp.split(mod, 6, axis=-1)
        h = rmsnorm(x, norm_mix[i]) * (1 + sc1) + sh1
        j = i // N_MIXERS
        if i % N_MIXERS == 0:
            y = windowed_gqa(h, a_w_in[j], a_w_out[j], a_sink[j])
        else:
            y = dilated_attention(h, b_w_in[j], b_w_out[j])
        x = x + g1 * y
        h = rmsnorm(x, norm_ffn[i]) * (1 + sc2) + sh2
        x = x + g2 * swiglu(h, ffn_w_in[i], ffn_w_out[i])
    return rmsnorm(x, final_norm)


DEPTH_2 = 1

MIX_WIDTH = D_MODEL
SSM_WIDTH = MIX_WIDTH // 2
CONV_WIDTH = MIX_WIDTH - SSM_WIDTH
SSM_GROUP = 16
SSM_N_GROUPS = SSM_WIDTH // SSM_GROUP
SSM_STATE = 64
CONV_HEAD_DIM = 64
CONV_N_HEADS = CONV_WIDTH // CONV_HEAD_DIM
CONV_K = 3
DT_MIN = 0.001
DT_MAX = 0.1
EPS = 1e-6
IN_COLS = 2 * SSM_WIDTH + 4 * CONV_WIDTH


def rmsnorm_2(x, g):
    x32 = x.astype(jnp.float32)
    y = x32 * lax.rsqrt(jnp.mean(x32 * x32, axis=-1, keepdims=True) + EPS)
    return (y * g.astype(jnp.float32)).astype(x.dtype)

def _scan_combine(c1, c2):
    a1r, a1i, b1r, b1i = c1
    a2r, a2i, b2r, b2i = c2
    ar = a2r * a1r - a2i * a1i
    ai = a2r * a1i + a2i * a1r
    br = a2r * b1r - a2i * b1i + b2r
    bi = a2r * b1i + a2i * b1r + b2i
    return (ar, ai, br, bi)

def s5_mixer(u, a_re, a_im, log_dt, b_re, b_im, c_re, c_im, d_skip, w_glu, b_glu):
    bsz, seq, _ = u.shape
    f32 = jnp.float32
    u32 = u.astype(f32).reshape(bsz, seq, SSM_N_GROUPS, SSM_GROUP)
    a_re = a_re.astype(f32); a_im = a_im.astype(f32)
    dt = jnp.exp(log_dt.astype(f32))[:, None]
    mag = jnp.exp(a_re * dt)
    ab_re = mag * jnp.cos(a_im * dt)
    ab_im = mag * jnp.sin(a_im * dt)
    den = a_re * a_re + a_im * a_im
    p_re = ab_re - 1.0
    p_im = ab_im
    q_re = (p_re * a_re + p_im * a_im) / den
    q_im = (p_im * a_re - p_re * a_im) / den
    b_re = b_re.astype(f32); b_im = b_im.astype(f32)
    bb_re = q_re[..., None] * b_re - q_im[..., None] * b_im
    bb_im = q_re[..., None] * b_im + q_im[..., None] * b_re
    bu_re = jnp.einsum('blgh,gph->blgp', u32, bb_re)
    bu_im = jnp.einsum('blgh,gph->blgp', u32, bb_im)
    a_seq_re = jnp.broadcast_to(ab_re[None, None], (1, seq, SSM_N_GROUPS, SSM_STATE))
    a_seq_im = jnp.broadcast_to(ab_im[None, None], (1, seq, SSM_N_GROUPS, SSM_STATE))
    _, _, s_re, s_im = lax.associative_scan(
        _scan_combine, (a_seq_re, a_seq_im, bu_re, bu_im), axis=1)
    y = (jnp.einsum('blgp,ghp->blgh', s_re, c_re.astype(f32))
         - jnp.einsum('blgp,ghp->blgh', s_im, c_im.astype(f32))
         + d_skip.astype(f32) * u32)
    y = y.reshape(bsz, seq, SSM_WIDTH)
    y = jax.nn.gelu(y)
    y = y * jax.nn.sigmoid(jnp.einsum('bld,de->ble', y, w_glu.astype(f32)) + b_glu.astype(f32))
    return y.astype(u.dtype)

def short_conv_mixer(h, gate_b, gate_c, conv_w):
    v = gate_c * h
    vp = jnp.pad(v, ((0, 0), (CONV_K - 1, 0), (0, 0)))
    seq = h.shape[1]
    y = sum(conv_w[k] * vp[:, k:k + seq] for k in range(CONV_K))
    return gate_b * y

def second_inputs(seed: int = 0) -> dict:
    key = jax.random.key(seed)
    ks = jax.random.split(key, 20)
    f32 = jnp.float32
    x = jax.random.normal(ks[0], (BATCH, SEQ, D_MODEL), f32)
    norm_gain = 1.0 + 0.02 * jax.random.normal(ks[1], (DEPTH_2, D_MODEL), f32)
    w_in = jax.random.normal(ks[2], (DEPTH_2, D_MODEL, IN_COLS), f32) * D_MODEL ** -0.5
    n = jnp.arange(SSM_STATE, dtype=f32)
    ssm_a_re = -0.5 + 0.01 * jax.random.normal(ks[3], (DEPTH_2, SSM_N_GROUPS, SSM_STATE), f32)
    ssm_a_im = math.pi * n + 0.01 * jax.random.normal(ks[4], (DEPTH_2, SSM_N_GROUPS, SSM_STATE), f32)
    ssm_log_dt = jax.random.uniform(ks[5], (DEPTH_2, SSM_N_GROUPS), f32,
                                    math.log(DT_MIN), math.log(DT_MAX))
    bscale = (2.0 * SSM_GROUP) ** -0.5
    ssm_b_re = jax.random.normal(ks[6], (DEPTH_2, SSM_N_GROUPS, SSM_STATE, SSM_GROUP), f32) * bscale
    ssm_b_im = jax.random.normal(ks[7], (DEPTH_2, SSM_N_GROUPS, SSM_STATE, SSM_GROUP), f32) * bscale
    cscale = (2.0 * SSM_STATE) ** -0.5
    ssm_c_re = jax.random.normal(ks[8], (DEPTH_2, SSM_N_GROUPS, SSM_GROUP, SSM_STATE), f32) * cscale
    ssm_c_im = jax.random.normal(ks[9], (DEPTH_2, SSM_N_GROUPS, SSM_GROUP, SSM_STATE), f32) * cscale
    ssm_d = 1.0 + 0.1 * jax.random.normal(ks[10], (DEPTH_2, SSM_N_GROUPS, SSM_GROUP), f32)
    w_glu = jax.random.normal(ks[11], (DEPTH_2, SSM_WIDTH, SSM_WIDTH), f32) * SSM_WIDTH ** -0.5
    b_glu = 0.01 * jax.random.normal(ks[12], (DEPTH_2, SSM_WIDTH), f32)
    conv_w = jax.random.normal(ks[13], (DEPTH_2, CONV_K, CONV_WIDTH), f32) * CONV_K ** -0.5
    w_out = jax.random.normal(ks[14], (DEPTH_2, MIX_WIDTH, D_MODEL), f32) * MIX_WIDTH ** -0.5
    final_norm_gain = 1.0 + 0.02 * jax.random.normal(ks[15], (D_MODEL,), f32)
    return {"x": x, "norm_gain": norm_gain, "w_in": w_in,
            "ssm_a_re": ssm_a_re, "ssm_a_im": ssm_a_im, "ssm_log_dt": ssm_log_dt,
            "ssm_b_re": ssm_b_re, "ssm_b_im": ssm_b_im,
            "ssm_c_re": ssm_c_re, "ssm_c_im": ssm_c_im, "ssm_d": ssm_d,
            "w_glu": w_glu, "b_glu": b_glu, "conv_w": conv_w, "w_out": w_out,
            "final_norm_gain": final_norm_gain}

def second_block(x, norm_gain, w_in, ssm_a_re, ssm_a_im, ssm_log_dt, ssm_b_re, ssm_b_im,
              ssm_c_re, ssm_c_im, ssm_d, w_glu, b_glu, conv_w, w_out, final_norm_gain):
    h = x
    for l in range(DEPTH_2):
        xn = rmsnorm_2(h, norm_gain[l])
        proj = jnp.einsum('bld,dc->blc', xn, w_in[l])
        s0 = SSM_WIDTH
        u_ssm = proj[..., :s0]
        z_ssm = proj[..., s0:2 * s0]
        c0 = 2 * s0
        h_conv = proj[..., c0:c0 + CONV_WIDTH]
        b_conv = proj[..., c0 + CONV_WIDTH:c0 + 2 * CONV_WIDTH]
        c_conv = proj[..., c0 + 2 * CONV_WIDTH:c0 + 3 * CONV_WIDTH]
        z_conv = proj[..., c0 + 3 * CONV_WIDTH:c0 + 4 * CONV_WIDTH]
        y_ssm = s5_mixer(u_ssm, ssm_a_re[l], ssm_a_im[l], ssm_log_dt[l],
                         ssm_b_re[l], ssm_b_im[l], ssm_c_re[l], ssm_c_im[l],
                         ssm_d[l], w_glu[l], b_glu[l]) * jax.nn.silu(z_ssm)
        y_conv = short_conv_mixer(h_conv, b_conv, c_conv, conv_w[l]) * jax.nn.silu(z_conv)
        y = jnp.concatenate([y_ssm, y_conv], axis=-1)
        h = h + jnp.einsum('blc,cd->bld', y, w_out[l])
    return rmsnorm_2(h, final_norm_gain)


def setup_inputs(seed=0):
    out = dict(first_inputs(seed))
    for name, value in second_inputs(seed + 1).items():
        if name != "x":
            out[name + "_2"] = value
    return out


def reference(
    x, c, ada_w, ada_b, norm_mix, norm_ffn, ffn_w_in, ffn_w_out, a_w_in, a_w_out, a_sink,
    b_w_in, b_w_out, final_norm, norm_gain_2, w_in_2, ssm_a_re_2, ssm_a_im_2, ssm_log_dt_2,
    ssm_b_re_2, ssm_b_im_2, ssm_c_re_2, ssm_c_im_2, ssm_d_2, w_glu_2, b_glu_2, conv_w_2,
    w_out_2, final_norm_gain_2,
):
    x = first_block(
        x, c, ada_w, ada_b, norm_mix, norm_ffn, ffn_w_in, ffn_w_out, a_w_in, a_w_out, a_sink,
        b_w_in, b_w_out, final_norm,
    )
    return second_block(
        x, norm_gain_2, w_in_2, ssm_a_re_2, ssm_a_im_2, ssm_log_dt_2, ssm_b_re_2, ssm_b_im_2,
        ssm_c_re_2, ssm_c_im_2, ssm_d_2, w_glu_2, b_glu_2, conv_w_2, w_out_2, final_norm_gain_2,
    )


_drawn_inputs = setup_inputs


def setup_inputs(seed=0):
    import zlib

    import numpy as np

    out = dict(_drawn_inputs(seed))
    spreads = {}
    factors = {'norm_mix': 4.277,
     'a_sink': 62.376,
     'norm_gain_2': 3.372,
     'ssm_a_re_2': 64.0,
     'ssm_a_im_2': 49.672,
     'ssm_log_dt_2': 51.712,
     'ssm_b_re_2': 64.0,
     'ssm_b_im_2': 64.0,
     'ssm_c_re_2': 64.0,
     'ssm_c_im_2': 64.0,
     'ssm_d_2': 3.426,
     'b_glu_2': 200.0,
     'final_norm_gain_2': 23.882}
    for name, (base, spread) in spreads.items():
        noise = np.random.default_rng([zlib.crc32(name.encode()), seed]).standard_normal(out[name].shape)
        drawn = base * np.exp(spread * noise) if base else spread * noise
        out[name] = jnp.asarray(drawn.astype(out[name].dtype))
    for name, factor in factors.items():
        out[name] = (out[name] * factor).astype(out[name].dtype)
    return out
```

```python
from contextlib import ExitStack

import concourse.bass as bass
import numpy as np
from concourse import mybir

F32 = mybir.dt.float32
I32 = mybir.dt.int32
ALU = mybir.AluOpType
ACT = mybir.ActivationFunctionType

P = 128
D = 1024
S = 1024
KC = D // P
ST = S // P
HALF = 512
DH = 64
FF = 2816
EPS = 1e-6
FAR = 1e32
LOWEST = -3.0e38
ROUND = 12582912.0

TURN_PARTS = (6.28125, 0.0019350051879882812, float(2 * np.pi - 6.28125 - 0.0019350051879882812))

SW = 512
NG, GC, NS = 32, 16, 64
NP = NG // 2
TB = 8
NB = S // TB


def slopes(n):
    return [float(np.float32(2.0 ** (-8.0 * (i + 1) / n))) for i in range(n)]


class Unit:

    def __init__(self, layer, head, group, dil, chunks, first, pad, slope):
        self.layer, self.head, self.group, self.dil = layer, head, group, dil
        self.chunks = chunks
        self.first = first
        self.pad = pad
        self.vtiles = ST + (1 if pad else 0)
        self.slope = slope

    def window(self, n):
        w = P * self.chunks
        length = S // self.dil
        if self.chunks == 1:
            return 0, w
        start = (n * P) % length
        lo = max(0, -(start + self.first))
        hi = min(w, length - start - self.first)
        return lo, hi

    def parts(self, n):
        lo, hi = self.window(n)
        shift = 0 if self.pad else self.first // P
        return [(c, n + c + shift) for c in range(self.chunks) if c * P < hi and (c + 1) * P > lo]


class Ledger:

    def __init__(self):
        self.used, self.freed, self.of = [0] * 4, [0] * 4, {}

    def add(self, name, d, frees=1):
        self.used[d] += 1
        self.of[name] = (d, self.used[d], self.freed[d])
        self.freed[d] += frees

    def block(self, name, counts, frees):
        self.of[name] = (list(self.used), list(self.freed))
        self.used = [a + b for a, b in zip(self.used, counts)]
        self.freed = [a + b for a, b in zip(self.freed, frees)]


class Stream:

    def __init__(self):
        self.last, self.dmas, self.of = [None] * 3, [0] * 3, {}

    def add(self, name, s, last, dmas=1):
        self.dmas[s] += dmas
        self.of[name] = (s, self.last[s], 16 * self.dmas[s])
        self.last[s] = last

    def block(self, name, n, lasts):
        self.of[name] = (list(self.last), list(self.dmas))
        self.last = list(lasts)
        self.dmas = [a + n for a in self.dmas]


NF = FF // 256
NORMS = 7
SSM_LOADS = 19


def gate_up_at(g):
    return 0 if g == 0 else 4 + 12 * (g - 1)


def down_at(g):
    return 8 + 12 * g if g < NF - 1 else 4 + 12 * (NF - 1)


def is_up(pos):
    return pos in (1, 3) or pos >= 4 and (pos - 4) % 12 in (1, 3) and pos < down_at(NF - 1)


def freed_at(pos):
    return sum(1 for p in range(pos % 3, pos, 3) if not is_up(p))


TURN = [sum(1 for p in range(4, 28) if p % 3 == d and not is_up(p)) for d in range(3)]


def units():
    a, b = slopes(16), slopes(24)
    out = [Unit(0, j, 0, 1, 3, -P, 0, a[4 * j:4 * j + 4]) for j in range(4)]
    for g, dil in enumerate((1, 4, 16)):
        for j in range(2):
            s = [dil * v for v in b[8 * g + 4 * j:8 * g + 4 * j + 4]]
            wide = dil < 16
            out.append(Unit(1, j, g, dil, 2 if wide else 1, -64 if wide else 0, 64 if wide else 0, s))
    return out


def plan_accumulators():
    use = Ledger()
    for t in range(2):
        use.add(("vectors", t), 3)
    for c in range(KC):
        use.add(("x", c), c % 3)

    def norm(n):
        use.add(("norm sum", n), 3)
        use.add(("norm spread", n), 2, frees=0)

    use.add(("ada", 0), 3)
    use.add(("ada", 1), 3)
    norm(0)
    for u in range(4):
        for what in ("q0", "q1", "kv", "v"):
            use.add((what, u), 0)
        if u > 0:
            use.add(("ada", 1 + u), 0)
    use.add(("ada", 5), 0)
    for m in range(KC):
        use.add(("wo", 0, m), m % 3)
    norm(1)
    ffn = [len(range(d, 12 * NF, 3)) for d in range(3)]
    ffn_frees = [freed_at(12 * NF + (d - 12 * NF) % 3) for d in range(3)]
    use.block(("ffn", 0), ffn + [6], ffn_frees + [6])
    norm(2)
    for u in range(4, 10):
        for what in ("q0", "q1", "kv", "v"):
            use.add((what, u), 0)
    for g in range(3):
        use.add(("lse", g), g)
    for m in range(4):
        for g in range(3):
            use.add(("alpha", m, g), (3 + 3 * m + g) % 4)
    for m in range(KC):
        use.add(("wo", 1, m), m % 3)
    norm(3)
    use.block(("ffn", 1), ffn + [1], ffn_frees + [1])
    for q in range(4):
        use.add(("win", q), q)
    for q in range(4):
        use.add(("lag", q), q)
    norm(4)
    norm(5)
    for j in range(4):
        for w in range(4):
            use.add(("conv", j, w), w)
    for what in ("z", "u", "u^T"):
        for e in range(4):
            use.add((what, e), e)
    for h in range(2):
        use.add(("w re", h), 2 * h)
        use.add(("w im", h), 2 * h + 1)
    for what in ("y", "y^T", "glu"):
        for e in range(4):
            use.add((what, e), e)
    for m in range(KC):
        use.add(("out", m), m % 3)
    norm(6)
    for t in range(ST):
        use.add(("store", t), t % 3)
    return use.of


def plan_weights():
    s = Stream()

    def mix(us):
        for u in us:
            s.add(("q", u), 0, ("q1", u))
            s.add(("kv", u), 1, ("kv", u), 2)

    def ffn(l):
        s.block(("ffn", l), NF, [("ffn", l, gate_up_at(NF - 1) + 2), ("ffn", l, gate_up_at(NF - 1) + 3), ("ffn", l, down_at(NF - 1) + 7)])

    mix(range(4))
    for n in range(4):
        s.add(("wo", 0, n), (2 + n) % 3, ("wo", 0, 2 * n + 1))
    ffn(0)
    mix(range(4, 10))
    for n in range(2):
        s.add(("wo", 1, n), (2 + n) % 3, ("wo", 1, 4 * n + 3))
    ffn(1)
    for j in range(4):
        s.add(("conv", j, 0), 0, ("conv", j, 1), 2)
        s.add(("conv", j, 1), 1, ("conv", j, 3), 2)
    rest = [(("z", n), ("z", 2 * n + 1)) for n in range(2)] + [(("u", n), ("u", 3)) for n in range(2)]
    rest += [(("glu",), ("glu", 3))] + [(("out", n), ("out", 2 * n + 1)) for n in range(4)]
    for n, (what, last) in enumerate(rest):
        s.add(what, (2 + n) % 3, last)
    return s.of


def two_blocks_kernel(nc, x, c, ada_w, ada_b, norm_mix, norm_ffn, ffn_w_in, ffn_w_out, a_w_in, a_w_out, a_sink,
                      b_w_in, b_w_out, final_norm, norm_gain_2, w_in_2, ssm_a_re_2, ssm_a_im_2, ssm_log_dt_2,
                      ssm_b_re_2, ssm_b_im_2, ssm_c_re_2, ssm_c_im_2, ssm_d_2, w_glu_2, b_glu_2, conv_w_2, w_out_2,
                      final_norm_gain_2, out):
    UNITS = units()
    ACC, WTS = plan_accumulators(), plan_weights()

    ctx = ExitStack()
    with ctx:
        def sb(name, shape, dt=F32):
            return ctx.enter_context(nc.sbuf_tensor(name, shape, dt))

        def sem(name):
            return ctx.enter_context(nc.semaphore(name))

        xT = sb("xT", [P, KC, S])
        hT = sb("hT", [P, KC, S])
        wpair = [sb(f"wpair{s}", [P, 2048]) for s in range(3)]
        ident = sb("ident", [P, P])
        ones = sb("ones", [P, 1])
        vec = sb("vec", [P, 176])
        cond = sb("cond", [P, KC])
        mod = sb("mod", [P, 2, 48])
        gain = sb("gain", [P, NORMS, KC])
        var = sb("var", [P, NORMS, ST])
        dev = sb("dev", [P, NORMS, ST])
        rst = sb("rst", [P, NORMS, 5, ST])
        sink = sb("sink", [P, 16])
        stat_m = sb("stat_m", [P, 48, 4])
        stat_n = sb("stat_n", [P, 48, 4])
        stat_l = sb("stat_l", [P, 48, 4])
        stat_s = sb("stat_s", [P, 32, 3, 4])
        stat_i = sb("stat_i", [P, 48, 4])
        pick = sb("pick", [8, 4, P])
        arena_words = 27900
        arena = sb("arena", [P, arena_words])
        psum = ctx.enter_context(nc.psum_tensor("psum", [P, 4096], F32))
        acc = [psum[:, 1024 * d:1024 * d + 1024] for d in range(4)]
        ADA_B, COND, GAINS, B_GLU, CONV_W = 0, 96, 104, 160, 164

        def places(*sizes):
            at, got = 0, []
            for n in sizes:
                got.append(arena[:, at:at + n])
                at += n
            assert at <= arena_words, (at, arena_words)
            return got

        LAY = []
        for layer, (n_out, width, keys, vals) in enumerate(((8, 384, S, 8), (12, 256, S + P, 9))):
            o_, q_, k_, vt_, v_, s_, p_, b_, d_, e_ = places(
                n_out * S, 4 * S, 2 * keys, keys, 2 * vals * DH, 8 * width, 8 * width, 8 * width, width, 0 if layer == 0 else P)
            LAY.append(dict(
                oT=o_.rearrange("p (m t) -> p m t", t=S), q=q_.rearrange("p (b m t) -> p b m t", b=2, m=2),
                k=k_.rearrange("p (b t) -> p b t", b=2), vT=vt_, v=v_.rearrange("p (b n d) -> p b n d", b=2, d=DH),
                s=s_.rearrange("p (b h w) -> p b h w", b=2, h=4), pt=p_.rearrange("p (b w) -> p b w", b=2),
                bias=b_.rearrange("p (b h w) -> p b h w", b=2, h=4), dist=d_, dist16=e_))
        a_end = 8192 + 4096 + 2048 + 1024 + 1024 + 3 * 3072 + 384
        ada_acc = arena[:, a_end:a_end + 1024]
        rows_in = arena[:, 20000:20256].rearrange("p (t f) -> p t f", t=2)
        oT_flat = LAY[0]["oT"].rearrange("p m t -> p (m t)")
        ada_start = oT_flat.rearrange("p (b k n) -> p b k n", b=2, k=KC)
        hid_, gate_, ada_ = places(4096, 2048, 8192)
        hid = hid_.rearrange("p (b m t) -> p b m t", b=2, m=2)
        gate_act = gate_.rearrange("p (m t) -> p m t", m=2)
        ada_ffn = ada_.rearrange("p (b k n) -> p b k n", b=2, k=KC)
        ada_mid = wpair[2][:, :].rearrange("p (k n) -> p k n", k=KC)
        lse = arena[:, 12288:12480].rearrange("p (g n h) -> p g n h", g=3, n=ST)
        loglen = arena[:, 12480:12672].rearrange("p (u n h) -> p u n h", u=6, n=ST)
        lseT = arena[0:8, 12672:15744].rearrange("p (g t) -> p g t", g=3)
        top = arena[0:8, 15744:16768]
        esum = arena[0:8, 16768:17792]
        mix_tmp = arena[:, 17792:17792 + 4096].rearrange("p (b t) -> p b t", b=4)
        yc_, t_, cp_, lag_, ph_, win_, zs_, small_ = places(4096, 2056, 4608, 4096, 4096, 4096, 4096, 750)
        y_conv = yc_.rearrange("p (e t) -> p e t", t=S)
        y_ssm = cp_[:, 0:4096].rearrange("p (e t) -> p e t", t=S)
        tmp = [t_[:, 0:1024], t_[:, 1024:2048]]
        conv_y, conv_v = t_[:, 0:1024], t_[:, 1024:2050]
        cpow = cp_.rearrange("p (r c j h) -> p r c j h", r=2, c=NP, j=TB + 1)
        lag = lag_.rearrange("p (g w) -> p g w", g=NG)
        phase = ph_.rearrange("p (r c b) -> p r c b", r=2, c=NP)
        win = win_.rearrange("p (c r s) -> p c r s", c=NP, r=2)
        zs = zs_.rearrange("p (e t) -> p e t", t=S)
        yT = ph_.rearrange("p (e t) -> p e t", t=S)
        h_flat = hT[:, :, :].rearrange("p k t -> p (k t)")
        u_blk = h_flat[:, 0:4096].rearrange("p (g i h) -> p i g h", g=NG, i=TB)
        uT = h_flat[:, 4096:8192].rearrange("p (g b) -> p g b", g=NG)
        turned = h_flat[:, 0:4096].rearrange("p (r c b) -> p r c b", r=2, c=NP)
        y_blk = h_flat[:, 0:4096].rearrange("p (j f) -> p j f", j=TB)
        s_prev = win_.rearrange("p (r c b) -> p r c b", r=2, c=NP)
        bpow = zs_.rearrange("p (r c i h) -> p r c i h", r=2, c=NP, i=TB)
        by_lag = yc_[0:GC, :].rearrange("p (g j h) -> p g j h", g=NG, j=TB)
        b_raw = lag_[:, 0:512].rearrange("p (r c h) -> p r c h", r=2, c=NP)
        c_raw = lag_[:, 512:1024].rearrange("p (r n s) -> p r n s", r=2, n=2)
        cm_tmp = [lag_[:, 1024 + 768 * i:1024 + 768 * (i + 1)] for i in range(4)]
        small_at = [0]

        def small(n=16):
            small_at[0] += n
            return small_[:, small_at[0] - n:small_at[0]]

        are, aim, ldt, d_in = small(), small(), small(), small(32)
        z_re, z_im, s_cos, s_sin, a_r, a_i = (small() for _ in range(6))
        in_r, in_i, mag, mag8 = (small() for _ in range(4))
        dt, angle, den, inv, st0, st1, st2, st3 = (small() for _ in range(8))
        turn_r, turn_i = small(7 * 16), small(7 * 16)

        small_landed = sem("small_landed")
        x_landed = sem("x_landed")
        const_ready = sem("const_ready")
        cond_ready = sem("cond_ready")
        w_landed = [sem(f"w_landed{s}") for s in range(3)]
        acc_ready = [sem(f"acc_ready{d}") for d in range(4)]
        acc_free = [sem(f"acc_free{d}") for d in range(4)]
        ada_landed = [sem(f"ada_landed{b}") for b in range(3)]
        ada_step = sem("ada_step")
        ada_read = sem("ada_read")
        dve_step = sem("dve_step")
        pool_step = sem("pool_step")
        squares = sem("squares")
        dev_ready = sem("dev_ready")
        rstd_ready = sem("rstd_ready")
        scaled = sem("scaled")
        h_ready = sem("h_ready")
        x_ready = sem("x_ready")
        k_ready = sem("k_ready")
        pad_ready = sem("pad_ready")
        bias_ready = sem("bias_ready")
        scores_ready = sem("scores_ready")
        scores_read = sem("scores_read")
        max_ready = sem("max_ready")
        sink_ready = sem("sink_ready")
        exp_ready = sem("exp_ready")
        p_ready = sem("p_ready")
        pt_ready = sem("pt_ready")
        pt_read = sem("pt_read")
        o_ready = sem("o_ready")
        o_read = sem("o_read")
        log_ready = sem("log_ready")
        lse_ready = sem("lse_ready")
        log_diff = sem("log_diff")
        share_exp = sem("share_exp")
        share_ready = sem("share_ready")
        mixed = sem("mixed")
        hid_ready = sem("hid_ready")
        ssm_landed = sem("ssm_landed")
        ssm_power = sem("ssm_power")
        ssm_exp = sem("ssm_exp")
        den_ready = sem("den_ready")
        inv_ready = sem("inv_ready")
        c_ready = sem("c_ready")
        powers_ready = sem("powers_ready")
        lag_ready = sem("lag_ready")
        lag_landed = sem("lag_landed")
        conv_tap = sem("conv_tap")
        conv_ready = sem("conv_ready")
        s_ready = sem("s_ready")
        glu_ready = sem("glu_ready")
        stored = sem("stored")

        block = ctx.enter_context(nc.Block())

        win_rows = [ffn_w_in[l].rearrange("(k p) n -> p k n", p=P) for l in range(2)]
        wout_rows = [ffn_w_out[l].rearrange("(f p) n -> p f n", p=P) for l in range(2)]
        mix_rows = [a_w_in[0].rearrange("(k p) n -> p k n", p=P), b_w_in[0].rearrange("(k p) n -> p k n", p=P)]
        wo_rows = [a_w_out[0].rearrange("(k p) n -> p k n", p=P), b_w_out[0].rearrange("(k p) n -> p k n", p=P)]
        ada_rows = [ada_w[l].rearrange("(k p) n -> p k n", p=P) for l in range(2)]
        in2_rows = w_in_2[0].rearrange("(k p) n -> p k n", p=P)
        glu_rows = w_glu_2[0].rearrange("(k p) n -> p k n", p=P)
        out2_rows = w_out_2[0].rearrange("(k p) n -> p k n", p=P)

        def mix_columns(u):
            a = UNITS[u]
            if a.layer == 0:
                return 256 * a.head, 1024 + DH * a.head, 1280 + DH * a.head
            g = 2 * a.group + a.head
            return 256 * g, 1536 + DH * g, 1920 + DH * g

        def acc_number(name):
            if name[0] == "ffn":
                used, _ = ACC[name[:2]]
                return name[2] % 3, used[name[2] % 3] + name[2] // 3 + 1
            return ACC[name][:2]

        def v_free(u):
            return ACC[("v", u)][2] + 1

        def by_dilation(ap, dil):
            return ap.rearrange("p (a r) -> p r a", r=dil)

        def in_sequence(ap, dil):
            return ap.rearrange("p (r a) -> p r a", r=dil)

        @block.sync
        def _(sp):
            def into(name):
                s, last, _ = WTS[name]
                if last:
                    d, number = acc_number(last)
                    sp.wait_ge(acc_ready[d], number)
                return wpair[s], w_landed[s]

            def load(name, rows, k):
                w, landed = into(name)
                sp.dma_start(w[:, :].rearrange("p (k n) -> p k n", k=k), rows).then_inc(landed, 16)

            def load_mix(u):
                cq, ck, cv = mix_columns(u)
                rows = mix_rows[UNITS[u].layer]
                load(("q", u), rows[:, :, cq:cq + 256], KC)
                w, landed = into(("kv", u))
                kv = w[:, 0:1024].rearrange("p (k n) -> p k n", k=KC)
                sp.dma_start(kv[:, :, 0:DH], rows[:, :, ck:ck + DH]).then_inc(landed, 16)
                sp.dma_start(kv[:, :, DH:P], rows[:, :, cv:cv + DH]).then_inc(landed, 16)

            def load_ffn(l):
                lasts, _ = WTS[("ffn", l)]
                used, _ = ACC[("ffn", l)]
                hid_before = 2 * NF * l

                def group(g, s):
                    if s == 2:
                        src, k = wout_rows[l][:, bass.ds(2 * g, 2), :], 2
                    else:
                        src, k = win_rows[l][:, :, bass.ds(256 * g + s * FF, 256)], KC
                    sp.dma_start(wpair[s][:, :].rearrange("p (k n) -> p k n", k=k), src).then_inc(w_landed[s], 16)

                for s in range(2):
                    d, number = acc_number(lasts[s])
                    sp.wait_ge(acc_ready[d], number)
                    group(0, s)
                with sp.Fori(0, NF // 2) as i:
                    for b in range(2):
                        sp.wait_ge(hid_ready, hid_before + 4 * i + (2 * b + 2))
                        group(2 * i + (b + 1), 0)
                        group(2 * i + (b + 1), 1)
                        sp.wait_ge(acc_ready[0], used[0] + 8 * i + (2 + 4 * b))
                        group(2 * i + b, 2)
                sp.wait_ge(acc_ready[0], used[0] + 4 * (NF - 1) + 2)
                group(NF - 1, 2)

            for n, (ap, r) in enumerate(((ada_b.rearrange("l (m f) -> (l m) f", f=P), 96), (c.rearrange("o (m f) -> (o m) f", f=P), 8))):
                sp.dma_start(rows_in[96 * n:96 * n + r, 0, :], ap).then_inc(small_landed, 16)
            at = 0
            for ap in (norm_mix[0:1], norm_ffn[0:1], norm_mix[1:2], norm_ffn[1:2]):
                sp.dma_start(rows_in[at:at + 8, 1, :], ap.rearrange("o (m f) -> (o m) f", f=P)).then_inc(small_landed, 16)
                at += 8
            for ap in (final_norm, norm_gain_2[0], final_norm_gain_2):
                sp.dma_start(rows_in[at:at + 8, 1, :], ap.rearrange("(m f) -> m f", f=P)).then_inc(small_landed, 16)
                at += 8
            sp.dma_start(rows_in[56:60, 1, :], b_glu_2[0].rearrange("(m f) -> m f", f=P)).then_inc(small_landed, 16)
            sp.dma_start(rows_in[60:72, 1, :], conv_w_2[0].rearrange("k (m f) -> (k m) f", f=P)).then_inc(small_landed, 16)
            sp.dma_start(sink[:, :], a_sink.to_broadcast([P, 16])).then_inc(small_landed, 16)
            sp.dma_start(hT[:, :, :], x[0].rearrange("(t p) d -> p t d", p=P)).then_inc(x_landed, 16)
            for u in range(4):
                load_mix(u)
            sp.wait_ge(ada_read, 20)
            for n in range(4):
                load(("wo", 0, n), wo_rows[0][:, :, 256 * n:256 * n + 256], KC)
            load_ffn(0)
            for u in range(4, 10):
                load_mix(u)
            for n in range(2):
                load(("wo", 1, n), wo_rows[1][:, :, 512 * n:512 * n + 512], 4)
            load_ffn(1)
            for j in range(4):
                for h, (first, second) in enumerate(((2, 4), (3, 5))):
                    w, landed = into(("conv", j, h))
                    two = w[:, :].rearrange("p (o k n) -> p o k n", o=2, k=KC)
                    for o, part in enumerate((first, second)):
                        at = SW * part + P * j
                        sp.dma_start(two[:, o], in2_rows[:, :, at:at + P]).then_inc(landed, 16)
            for n in range(2):
                load(("z", n), in2_rows[:, :, SW + 256 * n:SW + 256 * n + 256], KC)
            for n in range(2):
                load(("u", n), in2_rows[:, 4 * n:4 * n + 4, 0:SW], 4)
            load(("glu",), glu_rows, 4)
            for n in range(4):
                load(("out", n), out2_rows[:, :, 256 * n:256 * n + 256], KC)
            for t in range(ST):
                sp.wait_ge(acc_free[t % 3], ACC[("store", t)][2] + 1)
                sp.dma_start(out[0, P * t:P * t + P, :], arena[:, 1024 * t:1024 * t + 1024]).then_inc(stored, 16)
            sp.wait_ge(stored, 16 * ST)

        @block.gpsimd
        def _(pool):
            steps = [0]

            def after(ins):
                steps[0] += 1
                ins.then_inc(pool_step, 1)
                pool.wait_ge(pool_step, steps[0])

            after(nc.gpsimd.memset(ident[:, :], 0.0))
            nc.gpsimd.affine_select(out=ident[:, :], in_=ident[:, :], compare_op=ALU.not_equal, fill=1.0, base=0,
                                    pattern=[[-1, P]], channel_multiplier=1).then_inc(const_ready, 1)
            nc.gpsimd.memset(ones[:, :], 1.0).then_inc(const_ready, 1)

            def ada_load(l, first, n, dst, b):
                pool.dma_start(dst, ada_rows[l][:, :, bass.ds(first, n)]).then_inc(ada_landed[b], 16)

            for m in range(4):
                if m >= 2:
                    pool.wait_ge(ada_read, m - 1)
                ada_load(0, 512 * m, 512, ada_start[:, m % 2], m % 2)

            after(nc.gpsimd.memset(pick[:, :, :], 1.0))
            after(nc.gpsimd.affine_select(out=pick[:, :, :], in_=pick[:, :, :], compare_op=ALU.is_ge, fill=0.0, base=0,
                                          pattern=[[P, 4], [1, P]], channel_multiplier=-DH))
            nc.gpsimd.affine_select(out=pick[:, :, :], in_=pick[:, :, :], compare_op=ALU.is_ge, fill=0.0, base=DH - 1,
                                    pattern=[[-P, 4], [-1, P]], channel_multiplier=DH).then_inc(const_ready, 1)

            def distances(dist, spare, first, reach):
                w = dist.shape[-1]
                after(nc.gpsimd.iota(dist, pattern=[[1, w]], base=first, channel_multiplier=-1, allow_small_or_imprecise_dtypes=True))
                after(nc.gpsimd.iota(spare, pattern=[[-1, w]], base=-first, channel_multiplier=1, allow_small_or_imprecise_dtypes=True))
                after(nc.gpsimd.affine_select(out=dist, in_=dist, compare_op=ALU.is_ge, fill=0.0, base=first, pattern=[[1, w]], channel_multiplier=-1))
                after(nc.gpsimd.affine_select(out=spare, in_=spare, compare_op=ALU.is_ge, fill=0.0, base=-first, pattern=[[-1, w]], channel_multiplier=1))
                after(nc.gpsimd.tensor_tensor(dist, dist, spare, ALU.add))
                if reach:
                    after(nc.gpsimd.affine_select(out=dist, in_=dist, compare_op=ALU.is_ge, fill=FAR, base=first + reach,
                                                  pattern=[[1, w]], channel_multiplier=-1))
                    after(nc.gpsimd.affine_select(out=dist, in_=dist, compare_op=ALU.is_ge, fill=FAR, base=reach - first,
                                                  pattern=[[-1, w]], channel_multiplier=1))

            def bias_tables(u):
                a = UNITS[u]
                lay = LAY[a.layer]
                w = P * a.chunks
                src = lay["dist16"] if a.dil == 16 else lay["dist"]
                if u % 4 >= 2 or u >= 6:
                    pool.wait_ge(scores_read, 32 * (u - 1))
                for h in range(4):
                    nc.gpsimd.tensor_scalar(lay["bias"][:, u % 2, h, 0:w], src[:, 0:w], -a.slope[h], None, ALU.mult).then_inc(bias_ready, 1)

            distances(LAY[0]["dist"], LAY[0]["bias"][:, 0, 0, :], -P, P)
            bias_tables(0)
            bias_tables(1)
            for u in range(4):
                if u >= 1 and u + 1 < 4:
                    bias_tables(u + 1)
                for k in range(4):
                    m = 4 * u + k
                    if m:
                        pool.wait_ge(ada_read, 4 + m)
                    ada_load(0, 2048 + 256 * m, 256, ada_mid, 2)

            d, number = acc_number(("wo", 0, KC - 1))
            pool.wait_ge(acc_ready[d], number)
            for m in range(2):
                ada_load(1, 512 * m, 512, ada_ffn[:, m], m)
            with pool.Fori(0, NF // 2) as i:
                for b in range(2):
                    pool.wait_ge(ada_read, 2 * i + (21 + b))
                    ada_load(1, 1024 * i + (1024 + 512 * b), 512, ada_ffn[:, b], b)

            used, _ = ACC[("ffn", 0)]
            pool.wait_ge(acc_ready[3], used[3] + 6)
            lay = LAY[1]
            distances(lay["dist"], lay["bias"][:, 0, 0, :], -64, 64)
            distances(lay["dist16"], lay["bias"][:, 0, 0, 0:P], 0, 0)
            half = S // 16
            after(nc.gpsimd.affine_select(out=lay["dist16"][0:half, :], in_=lay["dist16"][0:half, :], compare_op=ALU.is_ge, fill=FAR,
                                          base=half - 1, pattern=[[-1, P]], channel_multiplier=0))
            after(nc.gpsimd.affine_select(out=lay["dist16"][half:P, :], in_=lay["dist16"][half:P, :], compare_op=ALU.is_ge, fill=FAR,
                                          base=-half, pattern=[[1, P]], channel_multiplier=0))
            nc.gpsimd.memset(lay["vT"][0:DH, 0:64], 0.0).then_inc(pad_ready, 1)
            nc.gpsimd.memset(lay["vT"][0:DH, 64 + S:P + S], 0.0).then_inc(pad_ready, 1)
            for u in range(4, 10):
                bias_tables(u)

            d, number = acc_number(("wo", 1, KC - 1))
            pool.wait_ge(acc_ready[d], number)
            for q in range(2):
                rows, groups = slice(NS * q, NS * q + NS), slice(NP * q, NP * q + NP)
                pool.dma_start(are[rows, :], ssm_a_re_2[0, groups].rearrange("c s -> s c"), allow_slow_non_contiguous=True).then_inc(ssm_landed, 16)
                pool.dma_start(aim[rows, :], ssm_a_im_2[0, groups].rearrange("c s -> s c"), allow_slow_non_contiguous=True).then_inc(ssm_landed, 16)
                pool.dma_start(ldt[rows, :], ssm_log_dt_2[:, groups].to_broadcast([NS, NP])).then_inc(ssm_landed, 16)
            pool.dma_start(d_in[0:GC, :], ssm_d_2[0].rearrange("g h -> h g"), allow_slow_non_contiguous=True).then_inc(ssm_landed, 16)
            for r, (b_ap, c_ap) in enumerate(((ssm_b_re_2, ssm_c_re_2), (ssm_b_im_2, ssm_c_im_2))):
                for q in range(2):
                    rows = slice(NS * q, NS * q + NS)
                    pool.dma_start(b_raw[rows, r], b_ap[0, NP * q:NP * q + NP].rearrange("c s h -> s c h")).then_inc(ssm_landed, 16)
                    for n in range(2):
                        eight = c_ap[0, NP * q + 8 * n:NP * q + 8 * n + 8]
                        pool.dma_start(c_raw[:, r, n, rows], eight.rearrange("c h s -> (c h) s")).then_inc(ssm_landed, 16)

            def ts(dst, a, s1, op0, s2=None, op1=None):
                after(nc.gpsimd.tensor_scalar(dst, a, s1, s2, op0, op1) if op1 else nc.gpsimd.tensor_scalar(dst, a, s1, None, op0))

            def tt(dst, a, b, op):
                after(nc.gpsimd.tensor_tensor(dst, a, b, op))

            def series(dst, z, coefficients):
                ts(dst, z, coefficients[0], ALU.mult)
                for v in coefficients[1:]:
                    ts(dst, dst, v, ALU.add)
                    tt(dst, dst, z, ALU.mult)

            def square(dst_re, dst_im, re, im):
                nc.gpsimd.tensor_tensor(st0, re, re, ALU.mult)
                nc.gpsimd.tensor_tensor(st1, im, im, ALU.mult)
                after(nc.gpsimd.tensor_tensor(st2, re, im, ALU.mult))
                nc.gpsimd.tensor_tensor(dst_re, st0, st1, ALU.subtract)
                after(nc.gpsimd.tensor_scalar(dst_im, st2, 2.0, None, ALU.mult))

            pool.wait_ge(ssm_landed, 16 * SSM_LOADS)
            tt(st0, are, are, ALU.mult)
            tt(st1, aim, aim, ALU.mult)
            nc.gpsimd.tensor_tensor(den, st0, st1, ALU.add).then_inc(den_ready, 1)
            pool.wait_ge(ssm_exp, 1)
            nc.gpsimd.tensor_tensor(st2, are, dt, ALU.mult).then_inc(ssm_power, 1)
            tt(angle, aim, dt, ALU.mult)
            ts(st0, angle, float(1 / (2 * np.pi)), ALU.mult, ROUND, ALU.add)
            ts(st0, st0, -ROUND, ALU.add)
            for part in TURN_PARTS:
                ts(st1, st0, -part, ALU.mult)
                tt(angle, angle, st1, ALU.add)
            ts(angle, angle, 0.25, ALU.mult)
            tt(st0, angle, angle, ALU.mult)
            series(z_im, st0, (1 / 362880, -1 / 5040, 1 / 120, -1 / 6))
            tt(z_im, z_im, angle, ALU.mult)
            tt(z_im, z_im, angle, ALU.add)
            series(z_re, st0, (-1 / 3628800, 1 / 40320, -1 / 720, 1 / 24, -0.5))
            for _ in range(2):
                tt(st0, z_im, z_re, ALU.mult)
                tt(st0, st0, z_im, ALU.add)
                tt(z_re, z_im, z_im, ALU.mult)
                ts(z_re, z_re, -2.0, ALU.mult)
                ts(z_im, st0, 2.0, ALU.mult)
            ts(z_re, z_re, 1.0, ALU.add)
            pool.wait_ge(ssm_exp, 2)
            tt(a_r, mag, z_re, ALU.mult)
            tt(a_i, mag, z_im, ALU.mult)
            ts(st3, a_r, -1.0, ALU.add)
            pool.wait_ge(inv_ready, 1)
            tt(st0, st3, are, ALU.mult)
            tt(st1, a_i, aim, ALU.mult)
            tt(st0, st0, st1, ALU.add)
            tt(in_r, st0, inv, ALU.mult)
            tt(st0, a_i, are, ALU.mult)
            tt(st1, st3, aim, ALU.mult)
            tt(st0, st0, st1, ALU.subtract)
            tt(in_i, st0, inv, ALU.mult)
            tt(mag8, mag, mag, ALU.mult)
            tt(mag8, mag8, mag8, ALU.mult)
            tt(mag8, mag8, mag8, ALU.mult)
            for _ in range(3):
                square(z_re, z_im, z_re, z_im)
            after(nc.gpsimd.tensor_copy(turn_r[:, 0:16], z_re))
            after(nc.gpsimd.tensor_copy(turn_i[:, 0:16], z_im))
            for n in range(1, 7):
                last, now = slice(16 * (n - 1), 16 * n), slice(16 * n, 16 * n + 16)
                square(turn_r[:, now], turn_i[:, now], turn_r[:, last], turn_i[:, last])

            def turns(ap, n):
                return ap.rearrange("p (c o) -> p c o", o=1).to_broadcast([P, NP, n])

            def cmul(out_re, out_im, xr, xi, yr, yi, minus=False):
                n = xr.shape[-1]
                t = [v[:, 0:NP * n].rearrange("p (c o) -> p c o", c=NP) for v in cm_tmp]
                nc.gpsimd.tensor_tensor(t[0], xr, yr, ALU.mult)
                nc.gpsimd.tensor_tensor(t[1], xi, yi, ALU.mult)
                nc.gpsimd.tensor_tensor(t[2], xr, yi, ALU.mult)
                after(nc.gpsimd.tensor_tensor(t[3], xi, yr, ALU.mult))
                nc.gpsimd.tensor_tensor(out_re, t[0], t[1], ALU.add if minus else ALU.subtract)
                after(nc.gpsimd.tensor_tensor(out_im, t[3], t[2], ALU.subtract if minus else ALU.add))

            cmul(bpow[:, 0, :, TB - 1, :], bpow[:, 1, :, TB - 1, :], b_raw[:, 0], b_raw[:, 1], turns(in_r, GC), turns(in_i, GC))
            for i in range(TB - 2, -1, -1):
                cmul(bpow[:, 0, :, i, :], bpow[:, 1, :, i, :], bpow[:, 0, :, i + 1, :], bpow[:, 1, :, i + 1, :], turns(a_r, GC), turns(a_i, GC))
            pool.wait_ge(c_ready, 1)
            pool.wait_ge(acc_free[3], ACC[("ffn", 1)][1][3] + 1)
            for j in range(TB):
                cmul(cpow[:, 0, :, j + 1, :], cpow[:, 1, :, j + 1, :], cpow[:, 0, :, j, :], cpow[:, 1, :, j, :], turns(a_r, GC), turns(a_i, GC), minus=True)
            nc.gpsimd.memset(phase[:, 0, :, 0:1], 1.0)
            after(nc.gpsimd.memset(phase[:, 1, :, 0:1], 0.0))
            for k in range(7):
                n = 2 ** k
                tr, ti = turn_r[:, 16 * k:16 * k + 16], turn_i[:, 16 * k:16 * k + 16]
                for at in range(0, n, 32):
                    m = min(32, n - at)
                    cmul(phase[:, 0, :, n + at:n + at + m], phase[:, 1, :, n + at:n + at + m],
                         phase[:, 0, :, at:at + m], phase[:, 1, :, at:at + m], turns(tr, m), turns(ti, m))
            nc.gpsimd.memset(lag_, 0.0).then_inc(powers_ready, 1)
            pool.wait_ge(powers_ready, 1)
            pool.wait_ge(lag_ready, 1)
            for i in range(TB):
                pool.dma_start(lag[GC * i:GC * i + GC, :, GC * i:P],
                               yc_[0:GC, :].rearrange("p (g w) -> p g w", g=NG)[:, :, 0:P - GC * i]).then_inc(lag_landed, 16)

        @block.tensor
        def _(pe):
            def take(name):
                d, number, freed = ACC[name]
                if freed:
                    pe.wait_ge(acc_free[d], freed)
                return acc[d], acc_ready[d]

            def weights(name):
                s, _, landed = WTS[name]
                pe.wait_ge(w_landed[s], landed)
                return wpair[s]

            def dense(dst, chunks, w, src, first=True, last=True):
                for n, k in enumerate(chunks):
                    for t in range(2):
                        mm = nc.tensor.matmul(dst[:, HALF * t:HALF * t + HALF], w(k), src(k)[:, HALF * t:HALF * t + HALF],
                                              start=first and n == 0, stop=last and n == len(chunks) - 1)
                return mm

            def norm(n):
                dst, ready = take(("norm sum", n))
                for k in range(KC):
                    pe.wait_ge(squares, KC * n + k + 1)
                    for t in range(ST):
                        mm = nc.tensor.matmul(dst[:, t:t + 1], hT[:, k, P * t:P * t + P], ones[:, :], start=k == 0 and t == 0,
                                              stop=k == KC - 1 and t == ST - 1, skip_group_check=True)
                mm.then_inc(ready, 1)
                dst, ready = take(("norm spread", n))
                pe.wait_ge(rstd_ready, n + 1)
                for t in range(ST):
                    mm = nc.tensor.matmul(dst[:, P * t:P * t + P], rst[:, n, 4, t:t + 1].to_broadcast([P, P]), ident[:, :], start=True, stop=True)
                mm.then_inc(ready, 1)

            def modulation(r, read):
                dst, ready = take(("ada", r))
                pe.wait_ge(ada_read, read)
                modulation_sums(dst).then_inc(ready, 1)

            def modulation_sums(dst):
                for m in range(KC):
                    mm = nc.tensor.matmul(dst[:, m:m + 1], ada_acc[:, P * m:P * m + P], ones[:, :], start=True, stop=True)
                return mm

            def project(u, part):
                lay = LAY[UNITS[u].layer]
                if part < 6:
                    name = (("q0", "q1", "kv")[part // 2], u)
                    if part % 2 == 0:
                        take(name)
                    d = ACC[name][0]
                    w = weights(("kv" if part >= 4 else "q", u))[:, :]
                    w = w[:, 0:1024].rearrange("p (k n) -> p k n", k=KC) if part >= 4 else w.rearrange("p (k n) -> p k n", k=KC)
                    at = P * (part // 2) if part < 4 else 0
                    first = part % 2 == 0
                    if u in (0, 4):
                        pe.wait_ge(h_ready, KC * (2 * UNITS[u].layer) + 4 * (part % 2) + 4)
                    mm = dense(acc[d], range(4 * (part % 2), 4 * (part % 2) + 4), lambda k: w[:, k, at:at + P], lambda k: hT[:, k, :],
                               first, not first)
                    if not first:
                        mm.then_inc(acc_ready[d], 1)
                if part == 7:
                    dst, ready = take(("v", u))
                    if u == 4:
                        pe.wait_ge(pad_ready, 2)
                    for n in range(UNITS[u].vtiles):
                        mm = nc.tensor.transpose(dst[:, DH * n:DH * n + DH], lay["vT"][0:DH, P * n:P * n + P], ident[0:DH, 0:DH])
                    mm.then_inc(ready, 1)

            def scores(t):
                u, n = t // 8, t % 8
                a, lay = UNITS[u], LAY[UNITS[u].layer]
                if n == 0:
                    pe.wait_ge(acc_free[0], ACC[("q1", u)][2] + 1)
                    pe.wait_ge(k_ready, 2 * (u + 1))
                lo, hi = a.window(n)
                key = P * n + a.first + a.pad
                for h in range(4):
                    e = 4 * t + h
                    if e >= 2:
                        pe.wait_ge(scores_read, e - 1)
                    rows = slice(DH * (h % 2), DH * (h % 2) + DH)
                    nc.tensor.matmul(acc[1][:, HALF * (e % 2) + lo:HALF * (e % 2) + hi], lay["q"][rows, u % 2, h // 2, P * n:P * n + P],
                                     lay["k"][rows, u % 2, key + lo:key + hi], start=True, stop=True).then_inc(scores_ready, 1)

            def turn(t):
                u, n = t // 8, t % 8
                lay = LAY[UNITS[u].layer]
                pe.wait_ge(p_ready, t + 1)
                if t:
                    pe.wait_ge(pt_read, t)
                for m, (c, _) in enumerate(UNITS[u].parts(n)):
                    for h in range(4):
                        mm = nc.tensor.transpose(psum[:, 2048 + HALF * m + P * h:2048 + HALF * m + P * h + P],
                                                 lay["s"][:, t % 2, h, P * c:P * c + P], ident[:, :])
                mm.then_inc(pt_ready, 1)

            def outputs(t):
                u, n = t // 8, t % 8
                lay = LAY[UNITS[u].layer]
                parts = UNITS[u].parts(n)
                if n == 0:
                    d, _, _ = ACC[("v", u)]
                    pe.wait_ge(acc_free[d], v_free(u))
                pe.wait_ge(pt_read, t + 1)
                if t:
                    pe.wait_ge(o_read, 2 * t)
                for m, (_, vt) in enumerate(parts):
                    mm = nc.tensor.matmul(psum[0:DH, 3584:4096], lay["v"][:, u % 2, vt, :], lay["pt"][:, t % 2, HALF * m:HALF * m + HALF],
                                          start=m == 0, stop=m == len(parts) - 1)
                mm.then_inc(o_ready, 1)

            def attention(first, last):
                for part in range(8):
                    project(first, part)
                for t in range(8 * first, 8 * last + 2):
                    if t < 8 * last:
                        scores(t)
                    if 8 * first <= t - 1 < 8 * last:
                        turn(t - 1)
                    if t - 2 >= 8 * first:
                        outputs(t - 2)
                    if t < 8 * last:
                        if t // 8 + 1 < last:
                            project(t // 8 + 1, t % 8)
                        if t % 8 == 7 and t < 32:
                            modulation(2 + t // 8, 4 + 4 * (t // 8 + 1))

            def ffn(l):
                used, freed = ACC[("ffn", l)]
                _, landed = WTS[("ffn", l)]

                def at(pos, i):
                    d = pos % 3
                    pe.wait_ge(acc_free[d], TURN[d] * i + (freed[d] + freed_at(pos)))
                    return acc[d], acc_ready[d]

                def gate_up(pos, g, i):
                    for n, (s, m) in enumerate(((0, 0), (1, 0), (0, 1), (1, 1))):
                        dst, ready = at(pos + n, i)
                        pe.wait_ge(w_landed[s], 16 * g + 16 * (landed[s] + 1))
                        w = wpair[s][:, :].rearrange("p (k n) -> p k n", k=KC)
                        dense(dst, range(KC), lambda k: w[:, k, P * m:P * m + P], lambda k: hT[:, k, :]).then_inc(ready, 1)

                def down(pos, g, b, i):
                    pe.wait_ge(w_landed[2], 16 * g + 16 * (landed[2] + 1))
                    pe.wait_ge(hid_ready, 2 * g + (2 * NF * l + 2))
                    w = wpair[2][:, :].rearrange("p (k n) -> p k n", k=2)
                    for m in range(KC):
                        if pos < down_at(NF - 1) and m in (0, 2):
                            pe.wait_ge(hid_ready, 2 * g + (2 * NF * l + 3 + m // 2))
                        dst, ready = at(pos + m, i)
                        dense(dst, range(2), lambda k: w[:, k, P * m:P * m + P], lambda k: hid[:, b, k, :]).then_inc(ready, 1)

                pe.wait_ge(h_ready, KC * (2 * l + 2))
                gate_up(0, 0, 0)
                if l == 0:
                    pe.wait_ge(acc_free[3], freed[3])
                    pe.wait_ge(ada_read, 22)
                    modulation_sums(acc[3]).then_inc(acc_ready[3], 1)
                else:
                    pe.wait_ge(ssm_landed, 16 * SSM_LOADS)
                    pe.wait_ge(acc_free[3], freed[3])
                    for r in range(2):
                        for n in range(2):
                            mm = nc.tensor.transpose(acc[3][:, 256 * r + P * n:256 * r + P * n + P], c_raw[:, r, n, :], ident[:, :])
                    mm.then_inc(acc_ready[3], 1)
                pe.wait_ge(hid_ready, 2 * NF * l + 2)
                with pe.Fori(0, NF // 2) as i:
                    for b in range(2):
                        gate_up(4 + 12 * b, 2 * i + (1 + b), i)
                        if l == 0 and b == 1:
                            pe.wait_ge(acc_free[3], i + (freed[3] + 1))
                            pe.wait_ge(ada_read, 2 * i + 24)
                            modulation_sums(acc[3]).then_inc(acc_ready[3], 1)
                        down(8 + 12 * b, 2 * i + b, b, i)
                down(down_at(NF - 1), NF - 1, 0, 0)

            pe.wait_ge(const_ready, 2)
            pe.wait_ge(small_landed, 16 * 12)
            for n, r in enumerate((104, 72)):
                dst, ready = take(("vectors", n))
                nc.tensor.transpose(dst[:, 0:r], rows_in[0:r, n, :], ident[0:r, 0:r]).then_inc(ready, 1)
            pe.wait_ge(x_landed, 16)
            for k in range(KC):
                dst, ready = take(("x", k))
                for t in range(ST):
                    mm = nc.tensor.transpose(dst[:, P * t:P * t + P], hT[:, t, P * k:P * k + P], ident[:, :])
                mm.then_inc(ready, 1)
            for r in range(2):
                modulation(r, 2 * r + 2)
            norm(0)
            attention(0, 4)
            pe.wait_ge(o_read, 64)
            for m in range(KC):
                dst, ready = take(("wo", 0, m))
                w = weights(("wo", 0, m // 2))[:, :].rearrange("p (k n) -> p k n", k=KC)
                dense(dst, range(KC), lambda k: w[:, k, P * (m % 2):P * (m % 2) + P], lambda k: LAY[0]["oT"][:, k, :]).then_inc(ready, 1)
            norm(1)
            ffn(0)
            norm(2)
            attention(4, 10)
            pe.wait_ge(lse_ready, 3)
            for g in range(3):
                dst, ready = take(("lse", g))
                for n in range(ST):
                    mm = nc.tensor.transpose(dst[0:8, P * n:P * n + P], lse[:, g, n, :], ident[:, :])
                mm.then_inc(ready, 1)
            for m in range(4):
                for g in range(3):
                    dst, ready = take(("alpha", m, g))
                    pe.wait_ge(share_ready, 1)
                    pe.wait_ge(const_ready, 3)
                    for t in range(2):
                        mm = nc.tensor.matmul(dst[:, HALF * t:HALF * t + HALF], pick[:, m, :], lseT[:, g, HALF * t:HALF * t + HALF], start=True, stop=True)
                    mm.then_inc(ready, 1)
            for m in range(KC):
                dst, ready = take(("wo", 1, m))
                w = weights(("wo", 1, m // 4))[:, :].rearrange("p (k n) -> p k n", k=4)
                pe.wait_ge(mixed, 4)
                dense(dst, range(4), lambda k: w[:, k, P * (m % 4):P * (m % 4) + P], lambda k: LAY[1]["oT"][:, k, :]).then_inc(ready, 1)
            norm(3)
            ffn(1)

            pe.wait_ge(powers_ready, 1)
            for q in range(4):
                dst, ready = take(("win", q))
                for k in range(4):
                    for r in range(2):
                        at = P * (2 * k + r)
                        mm = nc.tensor.transpose(dst[:, at:at + P], bpow[:, r, 4 * q + k, :, :], ident[:, :])
                mm.then_inc(ready, 1)
            for d in range(4):
                dst, ready = take(("lag", d))
                for k in range(8):
                    g = 8 * d + k
                    q, cc = g // NP, g % NP
                    rows = slice(NS * q, NS * q + NS)
                    for r in range(2):
                        mm = nc.tensor.matmul(dst[0:GC, P * k:P * k + P], bpow[rows, r, cc, TB - 1, :], cpow[rows, r, cc, 0:TB, :],
                                              start=r == 0, stop=r == 1)
                mm.then_inc(ready, 1)
            norm(4)
            norm(5)
            pe.wait_ge(h_ready, 40)
            for j in range(4):
                for n in range(4):
                    dst, ready = take(("conv", j, n))
                    w = weights(("conv", j, n // 2))[:, :].rearrange("p (o k n) -> p o k n", o=2, k=KC)
                    dense(dst, range(KC), lambda k: w[:, n % 2, k, :], lambda k: hT[:, k, :]).then_inc(ready, 1)
            for e in range(4):
                dst, ready = take(("z", e))
                w = weights(("z", e // 2))[:, :].rearrange("p (k n) -> p k n", k=KC)
                dense(dst, range(KC), lambda k: w[:, k, P * (e % 2):P * (e % 2) + P], lambda k: hT[:, k, :]).then_inc(ready, 1)
            w = [weights(("u", n))[:, :].rearrange("p (k n) -> p k n", k=4) for n in range(2)]
            for d in range(4):
                dst, ready = take(("u", d))
                for i in range(2):
                    for k in range(KC):
                        mm = nc.tensor.matmul(dst[:, HALF * i:HALF * i + HALF], hT[:, k, 2 * d + i::TB], w[k // 4][:, k % 4, :],
                                              start=k == 0, stop=k == KC - 1)
                mm.then_inc(ready, 1)
            for d in range(4):
                dst, ready = take(("u^T", d))
                pe.wait_ge(acc_free[d], ACC[("u", d)][2] + 1)
                if d == 0:
                    for dd in range(4):
                        pe.wait_ge(acc_free[dd], ACC[("u^T", dd)][2])
                for k in range(8):
                    g = 8 * d + k
                    mm = nc.tensor.transpose(dst[:, P * k:P * k + P], h_flat[:, P * g:P * g + P], ident[:, :])
                mm.then_inc(ready, 1)
            for h in range(2):
                for r, what in enumerate(("w re", "w im")):
                    dst, ready = take((what, h))
                    if h == 0 and r == 0:
                        for dd in range(4):
                            pe.wait_ge(acc_free[dd], ACC[("u^T", dd)][2] + 1)
                    for k in range(8):
                        cc = 8 * h + k
                        for q in range(2):
                            mm = nc.tensor.matmul(dst[NS * q:NS * q + NS, P * k:P * k + P], win[:, cc, r, NS * q:NS * q + NS],
                                                  uT[:, NP * q + cc, :], start=True, stop=True)
                    mm.then_inc(ready, 1)
            pe.wait_ge(lag_landed, 16 * TB)
            for d in range(4):
                dst, ready = take(("y", d))
                for k in range(8):
                    g = 8 * d + k
                    q, cc = g // NP, g % NP
                    rows = slice(NS * q, NS * q + NS)
                    nc.tensor.matmul(dst[:, P * k:P * k + P], uT[:, g, :], lag[:, g, :], start=True, stop=False)
                    if g == 0:
                        pe.wait_ge(s_ready, 4)
                    for r in range(2):
                        mm = nc.tensor.matmul(dst[:, P * k:P * k + P], s_prev[rows, r, cc, :], cpow[rows, r, cc, 1:TB + 1, :],
                                              start=False, stop=r == 1)
                mm.then_inc(ready, 1)
            for f in range(4):
                dst, ready = take(("y^T", f))
                if f == 0:
                    for dd in range(4):
                        pe.wait_ge(acc_free[dd], ACC[("y", dd)][2] + 1)
                for j in range(TB):
                    mm = nc.tensor.transpose(dst[:, P * j:P * j + P], y_blk[:, j, P * f:P * f + P], ident[:, :])
                mm.then_inc(ready, 1)
            w = weights(("glu",))[:, :].rearrange("p (k n) -> p k n", k=4)
            for e in range(4):
                dst, ready = take(("glu", e))
                if e == 0:
                    for dd in range(4):
                        pe.wait_ge(acc_free[dd], ACC[("y^T", dd)][2] + 1)
                dense(dst, range(4), lambda k: w[:, k, P * e:P * e + P], lambda k: yT[:, k, :]).then_inc(ready, 1)
            for m in range(KC):
                dst, ready = take(("out", m))
                w2 = weights(("out", m // 2))[:, :].rearrange("p (k n) -> p k n", k=KC)
                at = P * (m % 2)
                if m == 0:
                    pe.wait_ge(conv_ready, 4)
                dense(dst, range(4, 8), lambda k: w2[:, k, at:at + P], lambda k: y_conv[:, k - 4, :], True, False)
                if m == 0:
                    pe.wait_ge(glu_ready, 4)
                dense(dst, range(4), lambda k: w2[:, k, at:at + P], lambda k: y_ssm[:, k, :], False, True).then_inc(ready, 1)
            norm(6)
            pe.wait_ge(h_ready, 48)
            for t in range(ST):
                dst, ready = take(("store", t))
                for k in range(KC):
                    mm = nc.tensor.transpose(dst[:, P * k:P * k + P], hT[:, k, P * t:P * t + P], ident[:, :])
                mm.then_inc(ready, 1)

        @block.scalar
        def _(act):
            def ready(name):
                d, number = ACC[name][:2]
                act.wait_ge(acc_ready[d], number)
                return acc[d]

            def copied(name):
                d, _, freed = ACC[name]
                act.wait_ge(acc_free[d], freed + 1)

            def copy(dst, name, src=None, scale=1.0):
                a = ready(name)
                nc.scalar.activation(dst, a if src is None else src(a), ACT.Copy, scale=scale).then_inc(acc_free[ACC[name][0]], 1)

            def norm(n, wait_chunk):
                for k in range(KC):
                    wait_chunk(k)
                    nc.scalar.activation(hT[:, k, :], xT[:, k, :], ACT.Square).then_inc(squares, 1)
                act.wait_ge(acc_free[3], ACC[("norm sum", n)][2] + 1)
                nc.scalar.activation(dev[:, n, :], var[:, n, :], ACT.Sqrt).then_inc(dev_ready, 1)
                if n < 4:
                    l, at = n // 2, 24 * (n % 2)
                    for k in range(KC):
                        act.wait_ge(scaled, KC * n + k + 1)
                        nc.scalar.activation(hT[:, k, :], hT[:, k, :], ACT.Identity, bias=mod[:, l, at + k:at + k + 1]).then_inc(h_ready, 1)

            def queries(u, m):
                a = UNITS[u]
                q = LAY[a.layer]["q"]
                copy(in_sequence(q[:, u % 2, m, :], a.dil), (f"q{m}", u), lambda s: by_dilation(s, a.dil), 1 / 8)

            def exponentials(t):
                u, n = t // 8, t % 8
                a, lay = UNITS[u], LAY[UNITS[u].layer]
                ti = t if a.layer == 0 else t - 32
                lo, hi = a.window(n)
                if a.layer == 0:
                    act.wait_ge(sink_ready, t + 1)
                    nc.scalar.activation(stat_s[:, t, 1, :], stat_s[:, t, 0, :], ACT.Exp)
                act.wait_ge(max_ready, t + 1)
                for h in range(4):
                    s = lay["s"][:, t % 2, h, lo:hi]
                    e = nc.scalar.activation(s, s, ACT.Exp, bias=stat_n[:, ti, h:h + 1], accum_out=stat_l[:, ti, h:h + 1])
                e.then_inc(exp_ready, 1)

            def turned_copy(t):
                u, n = t // 8, t % 8
                cols = HALF * len(UNITS[u].parts(n))
                act.wait_ge(pt_ready, t + 1)
                if t >= 2:
                    act.wait_ge(o_ready, t - 1)
                nc.scalar.activation(LAY[UNITS[u].layer]["pt"][:, t % 2, 0:cols], psum[:, 2048:2048 + cols], ACT.Copy).then_inc(pt_read, 1)

            def attention(first, last):
                queries(first, 0)
                queries(first, 1)
                for t in range(8 * first, 8 * last + 1):
                    u, n = t // 8, t % 8
                    if u + 1 < last and n in (2, 4):
                        queries(u + 1, n // 2 - 1)
                    if t < 8 * last:
                        exponentials(t)
                    if t > 8 * first:
                        turned_copy(t - 1)

            def ffn(l):
                used, freed = ACC[("ffn", l)]

                def gates(pos, b, i, first=False):
                    for m in range(2):
                        at = pos + 2 * m
                        d = at % 3
                        if not first:
                            act.wait_ge(hid_ready, 4 * i + (2 * b + 2 * NF * l + m + 1))
                        act.wait_ge(acc_ready[d], 8 * i + (used[d] + at // 3 + 1))
                        nc.scalar.activation(gate_act[:, m, :], acc[d], ACT.Silu).then_inc(acc_free[d], 1)

                if l == 1:
                    act.wait_ge(ssm_landed, 16 * SSM_LOADS)
                    nc.scalar.activation(dt, ldt, ACT.Exp).then_inc(ssm_exp, 1)
                    act.wait_ge(ssm_power, 1)
                    nc.scalar.activation(mag, st2, ACT.Exp).then_inc(ssm_exp, 1)
                gates(0, 0, 0, True)
                with act.Fori(0, NF // 2) as i:
                    for b in range(2):
                        gates(4 + 12 * b, b, i)

            def ffn_done(l, k):
                used, freed = ACC[("ffn", l)]
                pos = down_at(NF - 1) + k
                act.wait_ge(acc_free[pos % 3], freed[pos % 3] + freed_at(pos) + 1)

            copied(("vectors", 0))
            nc.scalar.activation(cond[:, :], vec[:, COND:COND + KC], ACT.Silu).then_inc(cond_ready, 1)
            for k in range(1, KC, 2):
                copy(xT[:, k, :], ("x", k))
            ready(("x", KC - 1))
            norm(0, lambda k: copied(("x", k)))
            attention(0, 4)
            norm(1, lambda k: copied(("wo", 0, k)))
            ffn(0)
            norm(2, lambda k: ffn_done(0, k))
            attention(4, 10)
            act.wait_ge(p_ready, 80)
            nc.scalar.activation(loglen[:, :, :, :].rearrange("p u n h -> p (u n h)"), stat_l[:, :, :].rearrange("p t h -> p (t h)"), ACT.Ln).then_inc(log_ready, 1)
            act.wait_ge(log_diff, 3)
            nc.scalar.activation(lseT, lseT, ACT.Exp).then_inc(share_exp, 1)
            norm(3, lambda k: copied(("wo", 1, k)))
            ffn(1)
            norm(4, lambda k: ffn_done(1, k))
            norm(5, lambda k: act.wait_ge(x_ready, k + 1))

            for j in range(4):
                if j:
                    act.wait_ge(conv_ready, j)
                copy(conv_y, ("conv", j, 0))
                copied(("conv", j, 1))
                nc.scalar.activation(conv_y, conv_v[:, 0:S], ACT.Copy, scale=vec[:, CONV_W + j:CONV_W + j + 1]).then_inc(conv_tap, 1)
                copied(("conv", j, 2))
                nc.scalar.activation(conv_v[:, 2:2 + S], ready(("conv", j, 3)), ACT.Silu).then_inc(acc_free[3], 1)
            for e in range(4):
                nc.scalar.activation(zs[:, e, :], ready(("z", e)), ACT.Silu).then_inc(acc_free[e], 1)
            ready(("u", 3))
            for d in (0, 2):
                copy(u_blk[:, 2 * d:2 * d + 2], ("u", d), lambda s: s.rearrange("p (i g h) -> p i g h", i=2, g=NG))
            for d in (0, 2):
                copy(uT[:, 8 * d:8 * d + 8, :].rearrange("p g b -> p (g b)"), ("u^T", d))
            for d in range(4):
                src = ready(("y", d)).rearrange("p (g j h) -> p j g h", g=8, j=TB)
                nc.scalar.activation(y_blk[:, :, P * d:P * d + P].rearrange("p j (g h) -> p j g h", g=8), src,
                                     ACT.Gelu_apprx_tanh).then_inc(acc_free[d], 1)
            for f in (0, 2):
                copy(yT[:, f, :].rearrange("p (b j) -> p j b", j=TB), ("y^T", f), lambda s: s.rearrange("p (j b) -> p j b", j=TB))
            for e in range(4):
                if e >= 2:
                    act.wait_ge(glu_ready, e - 1)
                nc.scalar.activation(tmp[e % 2], ready(("glu", e)), ACT.Sigmoid, bias=vec[:, B_GLU + e:B_GLU + e + 1]).then_inc(acc_free[e], 1)
            norm(6, lambda k: copied(("out", k)))
            for t in range(0, ST, 2):
                copy(arena[:, S * t:S * t + S], ("store", t))

        @block.vector
        def _(dve):
            steps = [0]

            def after(ins):
                steps[0] += 1
                ins.then_inc(dve_step, 1)
                dve.wait_ge(dve_step, steps[0])

            def ready(name):
                d, number = ACC[name][:2]
                dve.wait_ge(acc_ready[d], number)
                return acc[d]

            def copied(name):
                d, _, freed = ACC[name]
                dve.wait_ge(acc_free[d], freed + 1)

            def free(name):
                return acc_free[ACC[name][0]]

            def copy(dst, name, src=None):
                a = ready(name)
                nc.vector.tensor_copy(dst, a if src is None else src(a)).then_inc(free(name), 1)

            def piece(buf, dst, landed, value, step, read):
                dve.wait_ge(landed, value)
                nc.vector.tensor_scalar(dst, buf[:, 0, :], cond[:, 0:1], None, ALU.mult).then_inc(ada_step, 1)
                for k in range(1, KC):
                    dve.wait_ge(ada_step, step + k)
                    nc.vector.scalar_tensor_tensor(dst, buf[:, k, :], cond[:, k:k + 1], dst, ALU.mult, ALU.add).then_inc(
                        ada_step if k < KC - 1 else ada_read, 1)

            def modulation(r):
                name = ("ada", r)
                nc.vector.tensor_tensor(mod[:, 0, 8 * r:8 * r + 8], ready(name)[:, 0:8], vec[:, 8 * r:8 * r + 8], ALU.add).then_inc(free(name), 1)

            def norm(n):
                a = ready(("norm sum", n))
                nc.vector.tensor_scalar(var[:, n, :], a[:, 0:ST], 1.0 / D, EPS, ALU.mult, ALU.add).then_inc(acc_free[3], 1)
                g = vec[:, GAINS + 8 * n:GAINS + 8 * n + 8]
                if n < 4:
                    l, at = n // 2, 24 * (n % 2) + 8
                    after(nc.vector.scalar_tensor_tensor(gain[:, n, :], mod[:, l, at:at + 8], 1.0, g, ALU.add, ALU.mult))
                else:
                    after(nc.vector.tensor_copy(gain[:, n, :], g))
                dve.wait_ge(dev_ready, n + 1)
                r = [rst[:, n, i, :] for i in range(5)]
                after(nc.vector.reciprocal(r[0], dev[:, n, :]))
                after(nc.vector.tensor_tensor(r[1], r[0], r[0], ALU.mult))
                after(nc.vector.tensor_tensor(r[2], r[1], var[:, n, :], ALU.mult))
                after(nc.vector.tensor_scalar(r[3], r[2], -0.5, 1.5, ALU.mult, ALU.add))
                nc.vector.tensor_tensor(r[4], r[0], r[3], ALU.mult).then_inc(rstd_ready, 1)
                spread = ready(("norm spread", n))
                for k in range(KC):
                    dst = xT if n == 4 else hT
                    done = scaled if n < 4 else x_ready if n == 4 else h_ready
                    nc.vector.scalar_tensor_tensor(dst[:, k, :], xT[:, k, :], gain[:, n, k:k + 1], spread, ALU.mult, ALU.mult).then_inc(done, 1)

            def keys_values(u):
                a, lay = UNITS[u], LAY[UNITS[u].layer]
                src = ready(("kv", u))
                for half in range(2):
                    dst = lay["k"][DH * half:DH * half + DH, u % 2, a.pad:a.pad + S]
                    nc.vector.tensor_copy(in_sequence(dst, a.dil), by_dilation(src[0:DH], a.dil)).then_inc(k_ready, 1)
                nc.vector.tensor_copy(in_sequence(lay["vT"][0:DH, a.pad:a.pad + S], a.dil), by_dilation(src[DH:P], a.dil)).then_inc(acc_free[0], 1)

            def values(u):
                a = UNITS[u]
                copy(LAY[a.layer]["v"][:, u % 2, 0:a.vtiles, :].rearrange("p n d -> p (n d)"), ("v", u), lambda s: s[:, 0:DH * a.vtiles])

            def biased(t):
                u, n = t // 8, t % 8
                a, lay = UNITS[u], LAY[UNITS[u].layer]
                ti = t if a.layer == 0 else t - 32
                lo, hi = a.window(n)
                if n == 0:
                    dve.wait_ge(bias_ready, 4 * (u + 1))
                if t >= 2:
                    dve.wait_ge(pt_ready, t - 1)
                if a.layer == 1 and a.chunks == 2:
                    if lo > 0:
                        nc.vector.memset(lay["s"][:, t % 2, :, 0:lo], 0.0)
                    if hi < P * a.chunks:
                        nc.vector.memset(lay["s"][:, t % 2, :, hi:P * a.chunks], 0.0)
                for h in range(4):
                    e = 4 * t + h
                    at = S + HALF * (e % 2)
                    start = sink[:, 4 * a.head + h:4 * a.head + h + 1] if a.layer == 0 else LOWEST
                    dve.wait_ge(scores_ready, e + 1)
                    nc.vector.tensor_tensor_reduce(out=lay["s"][:, t % 2, h, lo:hi], in0=psum[:, at + lo:at + hi], in1=lay["bias"][:, u % 2, h, lo:hi],
                                                   scale=1.0, scalar=start, op0=ALU.add, op1=ALU.max,
                                                   accum_out=stat_m[:, ti, h:h + 1]).then_inc(scores_read, 1)
                dve.wait_ge(scores_read, 4 * t + 4)
                nc.vector.tensor_scalar(stat_n[:, ti, :], stat_m[:, ti, :], -1.0, None, ALU.mult).then_inc(max_ready, 1)
                if a.layer == 0:
                    dve.wait_ge(max_ready, t + 1)
                    nc.vector.tensor_tensor(stat_s[:, t, 0, :], sink[:, 4 * a.head:4 * a.head + 4], stat_n[:, t, :], ALU.add).then_inc(sink_ready, 1)

            def normalised(t):
                u, n = t // 8, t % 8
                a, lay = UNITS[u], LAY[UNITS[u].layer]
                ti = t if a.layer == 0 else t - 32
                lo, hi = a.window(n)
                dve.wait_ge(exp_ready, t + 1)
                total = stat_l[:, ti, :]
                if a.layer == 0:
                    total = stat_s[:, t, 2, :]
                    after(nc.vector.tensor_tensor(total, stat_l[:, t, :], stat_s[:, t, 1, :], ALU.add))
                after(nc.vector.reciprocal(stat_i[:, ti, :], total))
                for h in range(4):
                    s = lay["s"][:, t % 2, h, lo:hi]
                    ins = nc.vector.tensor_scalar(s, s, stat_i[:, ti, h:h + 1], None, ALU.mult)
                ins.then_inc(p_ready, 1)

            def outputs(t):
                u, n = t // 8, t % 8
                a, lay = UNITS[u], LAY[UNITS[u].layer]
                m = 4 * a.group + 2 * a.head if a.layer == 1 else 2 * a.head
                dve.wait_ge(o_ready, t + 1)
                src = psum[0:DH, 3584:4096].rearrange("p (m r q) -> p m r q", m=2, r=2)
                for half in range(2):
                    dst, rows = lay["oT"][DH * half:DH * half + DH, m:m + 2, :], src[:, :, half, :]
                    if a.dil == 1:
                        dst = dst[:, :, P * n:P * n + P]
                    elif a.dil == 4:
                        dst = dst.rearrange("p m (a r) -> p m r a", r=4)[:, :, n // 2, P * (n % 2):P * (n % 2) + P]
                    else:
                        dst = dst.rearrange("p m (a r) -> p m r a", r=16)[:, :, 2 * n:2 * n + 2, :]
                        rows = rows.rearrange("p m (r a) -> p m r a", r=2)
                    nc.vector.tensor_copy(dst, rows).then_inc(o_read, 1)

            def attention(first, last):
                keys_values(first)
                for t in range(8 * first, 8 * last + 2):
                    u, n = t // 8, t % 8
                    if n == 0 and u < last:
                        values(u)
                        if 0 < u < 4:
                            modulation(1 + u)
                    if n == 6 and u + 1 < last:
                        keys_values(u + 1)
                    if t < 8 * last:
                        biased(t)
                    if 8 * first <= t - 1 < 8 * last:
                        normalised(t - 1)
                    if t - 2 >= 8 * first:
                        outputs(t - 2)
                    if t < 32 and n % 2 == 0:
                        m = 4 * u + n // 2
                        piece(ada_mid, ada_acc[:, 128 * n:128 * n + 256], ada_landed[2], 16 * (m + 1), 7 * (4 + m), 4 + m)

            def add_product(name, k, g):
                a = ready(name)
                ins = nc.vector.scalar_tensor_tensor(xT[:, k, :], a, g, xT[:, k, :], ALU.mult, ALU.add)
                ins.then_inc(free(name), 1)

            def ffn(l):
                used, freed = ACC[("ffn", l)]

                def hidden(pos, b, i):
                    for m in range(2):
                        gate, up = pos + 2 * m, pos + 2 * m + 1
                        dve.wait_ge(acc_free[gate % 3], TURN[gate % 3] * i + (freed[gate % 3] + freed_at(gate) + 1))
                        dve.wait_ge(acc_ready[up % 3], 8 * i + (used[up % 3] + up // 3 + 1))
                        nc.vector.tensor_tensor(hid[:, b, m, :], gate_act[:, m, :], acc[up % 3], ALU.mult).then_inc(hid_ready, 1)

                def down(pos, i):
                    for k in range(KC):
                        d, number = (pos + k) % 3, (pos + k) // 3
                        dve.wait_ge(acc_ready[d], 8 * i + (used[d] + number + 1))
                        nc.vector.scalar_tensor_tensor(xT[:, k, :], acc[d], mod[:, l, 40 + k:41 + k], xT[:, k, :], ALU.mult, ALU.add).then_inc(acc_free[d], 1)

                def next_modulation(m, b, i):
                    piece(ada_ffn[:, b], ada_acc[:, HALF * b:HALF * b + HALF], ada_landed[b], 16 * i + (48 + 16 * (m // 2)), 14 * i + 7 * (20 + m), 20 + m)

                def modulation_sums(i):
                    dve.wait_ge(acc_ready[3], i + (used[3] + 1))
                    at = 8 * i
                    nc.vector.tensor_tensor(mod[:, 1, bass.ds(at, 8)], acc[3][:, 0:8], vec[:, bass.ds(at + 48, 8)], ALU.add).then_inc(acc_free[3], 1)

                if l == 0:
                    next_modulation(0, 0, 0)
                    next_modulation(1, 1, 0)
                else:
                    dve.wait_ge(den_ready, 1)
                    nc.vector.reciprocal(inv, den).then_inc(inv_ready, 1)
                hidden(0, 0, 0)
                if l == 0:
                    modulation_sums(0)
                else:
                    dve.wait_ge(acc_ready[3], used[3] + 1)
                    c_rows = acc[3][:, 0:512].rearrange("p (r c h) -> p r c h", r=2, c=NP)
                    nc.vector.tensor_copy(cpow[:, 0, :, 0, :], c_rows[:, 0]).then_inc(c_ready, 1)
                    nc.vector.tensor_scalar(cpow[:, 1, :, 0, :], c_rows[:, 1], -1.0, None, ALU.mult).then_inc(acc_free[3], 1)
                with dve.Fori(0, NF // 2) as i:
                    for b in range(2):
                        hidden(4 + 12 * b, 1 - b, i)
                        if l == 0:
                            next_modulation(2 + b, b, i)
                            if b == 1:
                                modulation_sums(i + 1)
                        down(8 + 12 * b, i)
                down(down_at(NF - 1), 0)

            copy(vec[:, 0:104], ("vectors", 0), lambda s: s[:, 0:104])
            copy(vec[:, 104:176], ("vectors", 1), lambda s: s[:, 0:72])
            for k in range(0, KC, 2):
                copy(xT[:, k, :], ("x", k))
            dve.wait_ge(cond_ready, 1)
            for m in range(4):
                piece(ada_start[:, m % 2], ada_acc[:, HALF * (m % 2):HALF * (m % 2) + HALF], ada_landed[m % 2], 16 * (m // 2 + 1), 7 * m, m)
                if m % 2:
                    modulation(m // 2)
            for k in range(1, KC, 2):
                copied(("x", k))
            norm(0)
            dve.wait_ge(small_landed, 16 * 12)
            attention(0, 4)
            modulation(5)
            for k in range(KC):
                add_product(("wo", 0, k), k, mod[:, 0, 16 + k:17 + k])
            norm(1)
            ffn(0)
            norm(2)
            attention(4, 10)
            dve.wait_ge(log_ready, 1)
            for g in range(3):
                nc.vector.tensor_tensor(lse[:, g].rearrange("p n (j h) -> p j n h", j=2), loglen[:, 2 * g:2 * g + 2],
                                        stat_n[:, 16 * g:16 * g + 16, :].rearrange("p (j n) h -> p j n h", j=2), ALU.subtract).then_inc(lse_ready, 1)
            for g, dil in enumerate((1, 4, 16)):
                copy(by_dilation(lseT[:, g], dil), ("lse", g), lambda s: in_sequence(s[0:8], dil))
            for g in range(3):
                copied(("lse", g))
            after(nc.vector.tensor_tensor(top, lseT[:, 0], lseT[:, 1], ALU.max))
            after(nc.vector.tensor_tensor(top, top, lseT[:, 2], ALU.max))
            for g in range(3):
                nc.vector.tensor_tensor(lseT[:, g], lseT[:, g], top, ALU.subtract).then_inc(log_diff, 1)
            dve.wait_ge(share_exp, 1)
            after(nc.vector.tensor_tensor(esum, lseT[:, 0], lseT[:, 1], ALU.add))
            after(nc.vector.tensor_tensor(esum, esum, lseT[:, 2], ALU.add))
            after(nc.vector.reciprocal(esum, esum))
            for g in range(3):
                ins = nc.vector.tensor_tensor(lseT[:, g], lseT[:, g], esum, ALU.mult)
            ins.then_inc(share_ready, 1)
            for m in range(4):
                for g in range(3):
                    name = ("alpha", m, g)
                    nc.vector.tensor_tensor(mix_tmp[:, g], LAY[1]["oT"][:, 4 * g + m, :], ready(name), ALU.mult).then_inc(free(name), 1)
                copied(("alpha", m, 2))
                after(nc.vector.tensor_tensor(mix_tmp[:, 3], mix_tmp[:, 0], mix_tmp[:, 1], ALU.add))
                nc.vector.tensor_tensor(LAY[1]["oT"][:, m, :], mix_tmp[:, 3], mix_tmp[:, 2], ALU.add).then_inc(mixed, 1)
                dve.wait_ge(mixed, m + 1)
            for k in range(KC):
                add_product(("wo", 1, k), k, mod[:, 1, 16 + k:17 + k])
            norm(3)
            ffn(1)

            for q in range(4):
                copy(win[:, 4 * q:4 * q + 4].rearrange("p c r s -> p (c r s)"), ("win", q))
            for d in range(4):
                copy(by_lag[:, 8 * d:8 * d + 8].rearrange("p g j h -> p (g j h)"), ("lag", d), lambda s: s[0:GC])
            skip = tmp[0][0:GC, 0:NG * GC].rearrange("p (g h) -> p g h", g=NG)
            eye = ident[0:GC, 0:GC].rearrange("p (o h) -> p o h", o=1).to_broadcast([GC, NG, GC])
            after(nc.vector.tensor_tensor(skip, eye, d_in[0:GC, :].rearrange("p (g o) -> p g o", o=1).to_broadcast([GC, NG, GC]), ALU.mult))
            copied(("lag", 3))
            nc.vector.tensor_tensor(by_lag[:, :, 0, :], by_lag[:, :, 0, :], skip, ALU.add).then_inc(lag_ready, 1)
            norm(4)
            dve.wait_ge(x_ready, KC)
            norm(5)

            after(nc.vector.memset(conv_v[:, 0:2], 0.0))
            for j in range(4):
                def tap(k):
                    at = CONV_W + 4 * k + j
                    return vec[:, at:at + 1]

                copied(("conv", j, 0))
                nc.vector.tensor_tensor(conv_v[:, 2:2 + S], conv_y, ready(("conv", j, 1)), ALU.mult).then_inc(acc_free[1], 1)
                dve.wait_ge(conv_tap, j + 1)
                after(nc.vector.scalar_tensor_tensor(conv_y, conv_v[:, 1:1 + S], tap(1), conv_y, ALU.mult, ALU.add))
                after(nc.vector.scalar_tensor_tensor(conv_y, conv_v[:, 2:2 + S], tap(2), conv_y, ALU.mult, ALU.add))
                nc.vector.tensor_tensor(conv_y, conv_y, ready(("conv", j, 2)), ALU.mult).then_inc(acc_free[2], 1)
                copied(("conv", j, 3))
                dve.wait_ge(lag_landed, 16 * TB)
                nc.vector.tensor_tensor(y_conv[:, j, :], conv_y, conv_v[:, 2:2 + S], ALU.mult).then_inc(conv_ready, 1)
            ready(("u", 3))
            for d in (1, 3):
                copy(u_blk[:, 2 * d:2 * d + 2], ("u", d), lambda s: s.rearrange("p (i g h) -> p i g h", i=2, g=NG))
            for d in (1, 3):
                copy(uT[:, 8 * d:8 * d + 8, :].rearrange("p g b -> p (g b)"), ("u^T", d))

            def full(ap):
                return ap.rearrange("p (c b) -> p c b", b=NB)

            for h in range(2):
                c8 = slice(8 * h, 8 * h + 8)
                wr, wi = full(ready(("w re", h))), full(ready(("w im", h)))
                pc, ps = phase[:, 0, c8, :], phase[:, 1, c8, :]
                t0, t1 = full(tmp[0]), full(tmp[1])
                nc.vector.tensor_tensor(t0, wr, pc, ALU.mult)
                after(nc.vector.tensor_tensor(t1, wi, ps, ALU.mult))
                after(nc.vector.tensor_tensor(turned[:, 0, c8, :], t0, t1, ALU.add))
                nc.vector.tensor_tensor(t0, wr, ps, ALU.mult).then_inc(free(("w re", h)), 1)
                nc.vector.tensor_tensor(t1, wi, pc, ALU.mult).then_inc(free(("w im", h)), 1)
                copied(("w im", h))
                after(nc.vector.tensor_tensor(turned[:, 1, c8, :], t1, t0, ALU.subtract))
            for cc in range(NP):
                for r in range(2):
                    z = turned[:, r, cc, :]
                    ins = nc.vector.tensor_tensor_scan(z, mag8[:, cc:cc + 1].to_broadcast([P, NB]), z, 0.0, ALU.mult, ALU.add)
            after(ins)
            for r in range(2):
                ins = nc.vector.memset(s_prev[:, r, :, 0:1], 0.0)
            for h in range(2):
                c8 = slice(8 * h, 8 * h + 8)
                zr, zi = turned[:, 0, c8, 0:NB - 1], turned[:, 1, c8, 0:NB - 1]
                pc, ps = phase[:, 0, c8, 0:NB - 1], phase[:, 1, c8, 0:NB - 1]
                t0, t1 = full(tmp[0])[:, :, 0:NB - 1], full(tmp[1])[:, :, 0:NB - 1]
                for r, (p0, p1, op) in enumerate(((pc, ps, ALU.subtract), (ps, pc, ALU.add))):
                    nc.vector.tensor_tensor(t0, zr, p0, ALU.mult)
                    after(nc.vector.tensor_tensor(t1, zi, p1, ALU.mult))
                    nc.vector.tensor_tensor(s_prev[:, r, c8, 1:NB], t0, t1, op).then_inc(s_ready, 1)
                    dve.wait_ge(s_ready, 2 * h + r + 1)
            for f in (1, 3):
                copy(yT[:, f, :].rearrange("p (b j) -> p j b", j=TB), ("y^T", f), lambda s: s.rearrange("p (j b) -> p j b", j=TB))
            for e in range(4):
                if e % 2 == 0:
                    copied(("y^T", e))
                copied(("glu", e))
                after(nc.vector.tensor_tensor(tmp[e % 2], tmp[e % 2], yT[:, e, :], ALU.mult))
                nc.vector.tensor_tensor(y_ssm[:, e, :], tmp[e % 2], zs[:, e, :], ALU.mult).then_inc(glu_ready, 1)
            for m in range(KC):
                name = ("out", m)
                nc.vector.tensor_tensor(xT[:, m, :], xT[:, m, :], ready(name), ALU.add).then_inc(free(name), 1)
            norm(6)
            for t in range(1, ST, 2):
                copy(arena[:, S * t:S * t + S], ("store", t))


_INS = ["x", "c", "ada_w", "ada_b", "norm_mix", "norm_ffn", "ffn_w_in", "ffn_w_out", "a_w_in", "a_w_out", "a_sink", "b_w_in", "b_w_out",
        "final_norm", "norm_gain_2", "w_in_2", "ssm_a_re_2", "ssm_a_im_2", "ssm_log_dt_2", "ssm_b_re_2", "ssm_b_im_2", "ssm_c_re_2",
        "ssm_c_im_2", "ssm_d_2", "w_glu_2", "b_glu_2", "conv_w_2", "w_out_2", "final_norm_gain_2"]
_OUTS = [((1, 1024, 1024), "float32")]


def kernel(**inputs):
    import numpy as _np
    import concourse.bacc as _bacc
    from concourse import mybir as _mybir
    from concourse.bass_utils import run_bass_kernel_spmd as _run

    nc = _bacc.Bacc("TRN2", target_bir_lowering=False, num_devices=1)
    arrays, args = {}, []
    for name in _INS:
        a = _np.ascontiguousarray(inputs[name])
        arrays[f"in_{name}_dram"] = a
        args.append(nc.dram_tensor(f"in_{name}_dram", a.shape, _mybir.dt.from_np(a.dtype), kind="ExternalInput").ap())
    for i, (shape, dtype) in enumerate(_OUTS):
        dt = _mybir.dt.from_np(_np.dtype(dtype))
        args.append(nc.dram_tensor(f"out_{i}_dram", shape, dt, kind="ExternalOutput").ap())
    two_blocks_kernel(nc, *args)
    r = _run(nc, [arrays], core_ids=[0])
    return r.results[0]["out_0_dram"]
```

```python
from contextlib import ExitStack

import concourse.bass as bass
import numpy as np
from concourse import mybir

F32 = mybir.dt.float32
F32R = mybir.dt.float32r
ALU = mybir.AluOpType
ACT = mybir.ActivationFunctionType

P = 128
D = 1024
S = 1024
KC = D // P
ST = S // P
HALF = 512
DH = 64
FF = 2816
EPS = 1e-6
FAR = 1e32
LOWEST = -3.0e38
ROUND = 12582912.0

TURN_PARTS = (6.28125, 0.0019350051879882812, float(2 * np.pi - 6.28125 - 0.0019350051879882812))

SW = 512
NG, GC, NS = 32, 16, 64
NP = NG // 2
TB = 8
NB = S // TB


def slopes(n):
    return [float(np.float32(2.0 ** (-8.0 * (i + 1) / n))) for i in range(n)]


class Unit:

    def __init__(self, layer, head, group, dil, chunks, first, pad, slope):
        self.layer, self.head, self.group, self.dil = layer, head, group, dil
        self.chunks = chunks
        self.first = first
        self.pad = pad
        self.vtiles = ST + (1 if pad else 0)
        self.slope = slope

    def window(self, n):
        w = P * self.chunks
        length = S // self.dil
        if self.chunks == 1:
            return 0, w
        start = (n * P) % length
        lo = max(0, -(start + self.first))
        hi = min(w, length - start - self.first)
        return lo, hi

    def parts(self, n):
        lo, hi = self.window(n)
        shift = 0 if self.pad else self.first // P
        return [(c, n + c + shift) for c in range(self.chunks) if c * P < hi and (c + 1) * P > lo]


class Ledger:

    def __init__(self):
        self.used, self.freed, self.of = [0] * 4, [0] * 4, {}

    def add(self, name, d, frees=1):
        self.used[d] += 1
        self.of[name] = (d, self.used[d], self.freed[d])
        self.freed[d] += frees

    def block(self, name, counts, frees):
        self.of[name] = (list(self.used), list(self.freed))
        self.used = [a + b for a, b in zip(self.used, counts)]
        self.freed = [a + b for a, b in zip(self.freed, frees)]


class Stream:

    def __init__(self):
        self.last, self.dmas, self.of = [None] * 3, [0] * 3, {}

    def add(self, name, s, last, dmas=1):
        self.dmas[s] += dmas
        self.of[name] = (s, self.last[s], 16 * self.dmas[s])
        self.last[s] = last

    def block(self, name, counts, lasts):
        self.of[name] = (list(self.last), list(self.dmas))
        self.last = list(lasts)
        self.dmas = [a + n for a, n in zip(self.dmas, counts)]


NF = FF // 256
LOADS = (NF + 1, NF, NF - 1)
NORMS = 7
SSM_LOADS = 19


def gate_up_at(g):
    return 0 if g == 0 else 4 + 12 * (g - 1)


def down_at(g):
    return 8 + 12 * g if g < NF - 1 else 4 + 12 * (NF - 1)


def is_up(pos):
    return pos in (2, 3) or pos >= 4 and (pos - 4) % 12 in (2, 3) and pos < down_at(NF - 1)


def freed_at(pos):
    return sum(1 for p in range(pos % 3, pos, 3) if not is_up(p))


TURN = [sum(1 for p in range(4, 28) if p % 3 == d and not is_up(p)) for d in range(3)]


def units():
    a, b = slopes(16), slopes(24)
    out = [Unit(0, j, 0, 1, 3, -P, 0, a[4 * j:4 * j + 4]) for j in range(4)]
    for g, dil in enumerate((1, 4, 16)):
        for j in range(2):
            s = [dil * v for v in b[8 * g + 4 * j:8 * g + 4 * j + 4]]
            wide = dil < 16
            out.append(Unit(1, j, g, dil, 2 if wide else 1, -64 if wide else 0, 64 if wide else 0, s))
    return out


def plan_accumulators():
    use = Ledger()
    use.add(("vectors", 0), 3)
    for c in range(KC):
        use.add(("x", c), c % 3)

    def norm(n):
        use.add(("norm sum", n), 3)
        use.add(("norm spread", n), 2, frees=0)

    norm(0)
    use.add(("ada", 0), 3)
    use.add(("ada", 1), 3)
    use.add(("vectors", 1), 3)
    for u in range(4):
        for what in ("q0", "q1", "kv", "v"):
            use.add((what, u), 0)
        if u > 0:
            use.add(("ada", 1 + u), 0)
    use.add(("ada", 5), 0)
    for m in range(KC):
        use.add(("wo", 0, m), m % 3)
    use.add(("next ada",), 3)
    norm(1)
    ffn = [len(range(d, 12 * NF, 3)) for d in range(3)]
    ffn_frees = [freed_at(12 * NF + (d - 12 * NF) % 3) for d in range(3)]
    use.block(("ffn", 0), ffn + [5], ffn_frees + [5])
    norm(2)
    for u in range(4, 10):
        for what in ("q0", "q1", "kv", "v"):
            use.add((what, u), 0)
    for g in range(3):
        use.add(("lse", g), g)
    for m in range(4):
        for g in range(3):
            use.add(("alpha", m, g), (3 + 3 * m + g) % 4)
    for m in range(KC):
        use.add(("wo", 1, m), m % 3)
    norm(3)
    use.block(("ffn", 1), ffn + [0], ffn_frees + [0])
    norm(4)
    norm(5)
    for j in range(4):
        for w in range(4):
            use.add(("conv", j, w), w)
        if j == 0:
            use.add(("c^T",), 3)
    for what in ("win", "lag", "z", "u", "u^T"):
        for e in range(4):
            use.add((what, e), e)
    for h in range(2):
        use.add(("w re", h), 2 * h)
        use.add(("w im", h), 2 * h + 1)
    for what in ("y", "y^T", "glu"):
        for e in range(4):
            use.add((what, e), e)
    for m in range(KC):
        use.add(("out", m), m % 3)
    norm(6)
    for t in range(ST):
        use.add(("store", t), t % 3)
    return use.of


def plan_weights():
    s = Stream()

    def mix(us):
        for u in us:
            s.add(("q", u), 0, ("q1", u))
            s.add(("kv", u), 1, ("kv", u), 2)

    def ffn(l):
        lasts = (down_at(NF - 1) + KC - 1, gate_up_at(NF - 1) + 3, down_at(NF - 2) + KC - 1)
        s.block(("ffn", l), LOADS, [("ffn", l, pos) for pos in lasts])

    mix(range(4))
    for n in range(4):
        s.add(("wo", 0, n), (2 + n) % 3, ("wo", 0, 2 * n + 1))
    ffn(0)
    mix(range(4, 10))
    s.last[2] = ("kv", 9)
    for n in range(2):
        s.add(("wo", 1, n), (2 + n) % 3, ("wo", 1, 4 * n + 3))
    ffn(1)
    for j in range(4):
        s.add(("conv", j, 0), 0, ("conv", j, 1), 2)
        s.add(("conv", j, 1), 1, ("conv", j, 3), 2)
    rest = [(("z", n), ("z", 2 * n + 1)) for n in range(2)] + [(("u", n), ("u", 3)) for n in range(2)]
    rest += [(("glu",), ("glu", 3))] + [(("out", n), ("out", 2 * n + 1)) for n in range(4)]
    for n, (what, last) in enumerate(rest):
        s.add(what, (2 + n) % 3, last)
    return s.of


def two_blocks_kernel(nc, x, c, ada_w, ada_b, norm_mix, norm_ffn, ffn_w_in, ffn_w_out, a_w_in, a_w_out, a_sink,
                      b_w_in, b_w_out, final_norm, norm_gain_2, w_in_2, ssm_a_re_2, ssm_a_im_2, ssm_log_dt_2,
                      ssm_b_re_2, ssm_b_im_2, ssm_c_re_2, ssm_c_im_2, ssm_d_2, w_glu_2, b_glu_2, conv_w_2, w_out_2,
                      final_norm_gain_2, out):
    UNITS = units()
    ACC, WTS = plan_accumulators(), plan_weights()

    ctx = ExitStack()
    with ctx:
        def sb(name, shape, dt=F32):
            return ctx.enter_context(nc.sbuf_tensor(name, shape, dt))

        def sem(name):
            return ctx.enter_context(nc.semaphore(name))

        with ExitStack() as parts:
            def part(name, shape):
                return parts.enter_context(nc.sbuf_tensor(name, shape, F32R))

            hT_high = part("hT_high", [P, KC, S])
            h_low_mix = part("h_low_mix", [P, KC, S])
            w_low = [part(f"w_low{s}", [P, 2048]) for s in range(3)]
            hid_low = part("hid_low", [P, 2, 2, S])
            hid_high = part("hid_high", [P, 2, 2, S])
            part("gate_place", [P, 2, S])
            w_high = part("w_high", [P, 3, 2048])
            h_low = part("h_low", [P, KC, S])

        hT = sb("hT", [P, KC, S])
        xT = sb("xT", [P, KC, S])
        wpair = [sb(f"wpair{s}", [P, 2048]) for s in range(3)]
        arena_words = 27900
        arena = sb("arena", [P, arena_words])
        ident = sb("ident", [P, P])
        ones = sb("ones", [P, 1])
        vec = sb("vec", [P, 176])
        cond = sb("cond", [P, KC])
        mod = sb("mod", [P, 2, 48])
        gain = sb("gain", [P, NORMS, KC])
        var = sb("var", [P, NORMS, ST])
        dev = sb("dev", [P, NORMS, ST])
        rst = sb("rst", [P, NORMS, 5, ST])
        sink = sb("sink", [P, 16])
        stat_m = sb("stat_m", [P, 48, 4])
        stat_n = sb("stat_n", [P, 48, 4])
        stat_l = sb("stat_l", [P, 48, 4])
        stat_s = sb("stat_s", [P, 32, 3, 4])
        stat_i = sb("stat_i", [P, 48, 4])
        pick = sb("pick", [8, 4, P])
        psum = ctx.enter_context(nc.psum_tensor("psum", [P, 4096], F32))
        acc = [psum[:, 1024 * d:1024 * d + 1024] for d in range(4)]
        ADA_B, COND, GAINS, B_GLU, CONV_W = 0, 96, 104, 160, 164

        def places(*sizes):
            at, got = 0, []
            for n in sizes:
                got.append(arena[:, at:at + n])
                at += n
            assert at <= arena_words, (at, arena_words)
            return got

        LAY = []
        for layer, (n_out, width, keys, vals) in enumerate(((8, 384, S, 8), (12, 256, S + P, 9))):
            o_, q_, k_, vt_, v_, s_, p_, b_, d_, e_ = places(
                n_out * S, 4 * S, 2 * keys, keys, 2 * vals * DH, 8 * width, 8 * width, 8 * width, width, 0 if layer == 0 else P)
            LAY.append(dict(
                oT=o_.rearrange("p (m t) -> p m t", t=S), q=q_.rearrange("p (b m t) -> p b m t", b=2, m=2),
                k=k_.rearrange("p (b t) -> p b t", b=2), vT=vt_, v=v_.rearrange("p (b n d) -> p b n d", b=2, d=DH),
                s=s_.rearrange("p (b h w) -> p b h w", b=2, h=4), pt=p_.rearrange("p (b w) -> p b w", b=2),
                bias=b_.rearrange("p (b h w) -> p b h w", b=2, h=4), dist=d_, dist16=e_))
        a_end = 8192 + 4096 + 2048 + 1024 + 1024 + 3 * 3072 + 384
        ada_acc = arena[:, a_end:a_end + 1024]
        rows_in = arena[:, 20000:20256].rearrange("p (t f) -> p t f", t=2)
        ada_start = arena[:, 0:16384].rearrange("p (b k n) -> p b k n", b=4, k=KC)
        low_, _, gate_, _, hlow_, ada_sum, ada_ = places(4096, 4096, 2048, 6144, 8192, 1024, 2048)
        hid = low_.rearrange("p (b m t) -> p b m t", b=2, m=2)
        gate_act = gate_.rearrange("p (m t) -> p m t", m=2)
        h_whole = hlow_.rearrange("p (k t) -> p k t", k=KC)
        h_whole_mix = arena[:, 0:8192].rearrange("p (k t) -> p k t", k=KC)
        x_kept = out[0].rearrange("(p a) d -> p a d", p=P)
        ada_ffn = ada_.rearrange("p (b n) -> p b n", b=2)
        ada_mid = wpair[2][:, :].rearrange("p (k n) -> p k n", k=KC)
        lse = arena[:, 12288:12480].rearrange("p (g n h) -> p g n h", g=3, n=ST)
        loglen = arena[:, 12480:12672].rearrange("p (u n h) -> p u n h", u=6, n=ST)
        lseT = arena[0:8, 12672:15744].rearrange("p (g t) -> p g t", g=3)
        top = arena[0:8, 15744:16768]
        esum = arena[0:8, 16768:17792]
        mix_tmp = arena[:, 17792:17792 + 4096].rearrange("p (b t) -> p b t", b=4)
        yc_, t_, cp_, lag_, ph_, win_, zs_, small_ = places(4096, 2056, 4608, 4096, 4096, 4096, 4096, 750)
        y_conv = yc_.rearrange("p (e t) -> p e t", t=S)
        y_ssm = cp_[:, 0:4096].rearrange("p (e t) -> p e t", t=S)
        tmp = [t_[:, 0:1024], t_[:, 1024:2048]]
        conv_y, conv_v = t_[:, 0:1024], t_[:, 1024:2050]
        cpow = cp_.rearrange("p (r c j h) -> p r c j h", r=2, c=NP, j=TB + 1)
        lag = lag_.rearrange("p (g w) -> p g w", g=NG)
        phase = ph_.rearrange("p (r c b) -> p r c b", r=2, c=NP)
        win = win_.rearrange("p (c r s) -> p c r s", c=NP, r=2)
        zs = zs_.rearrange("p (e t) -> p e t", t=S)
        yT = ph_.rearrange("p (e t) -> p e t", t=S)
        h_flat = hT[:, :, :].rearrange("p k t -> p (k t)")
        u_blk = h_flat[:, 0:4096].rearrange("p (g i h) -> p i g h", g=NG, i=TB)
        uT = h_flat[:, 4096:8192].rearrange("p (g b) -> p g b", g=NG)
        turned = h_flat[:, 0:4096].rearrange("p (r c b) -> p r c b", r=2, c=NP)
        y_blk = h_flat[:, 0:4096].rearrange("p (j f) -> p j f", j=TB)
        s_prev = win_.rearrange("p (r c b) -> p r c b", r=2, c=NP)
        bpow = zs_.rearrange("p (r c i h) -> p r c i h", r=2, c=NP, i=TB)
        by_lag = t_[0:GC, 0:2048].rearrange("p (g j h) -> p g j h", g=NP, j=TB)
        b_raw = lag_[:, 0:512].rearrange("p (r c h) -> p r c h", r=2, c=NP)
        c_raw = lag_[:, 512:1024].rearrange("p (r n s) -> p r n s", r=2, n=2)
        cm_tmp = [lag_[:, 1024 + 768 * i:1024 + 768 * (i + 1)] for i in range(4)]
        small_at = [0]

        def small(n=16):
            small_at[0] += n
            return small_[:, small_at[0] - n:small_at[0]]

        are, aim, ldt, d_in = small(), small(), small(), small(32)
        z_re, z_im, s_cos, s_sin, a_r, a_i = (small() for _ in range(6))
        in_r, in_i, mag, mag8 = (small() for _ in range(4))
        dt, angle, den, inv, st0, st1, st2, st3 = (small() for _ in range(8))
        turn_r, turn_i = small(7 * 16), small(7 * 16)

        cond_landed = sem("cond_landed")
        small_landed = sem("small_landed")
        x_landed = sem("x_landed")
        const_ready = sem("const_ready")
        cond_ready = sem("cond_ready")
        w_landed = [sem(f"w_landed{s}") for s in range(3)]
        acc_ready = [sem(f"acc_ready{d}") for d in range(4)]
        acc_free = [sem(f"acc_free{d}") for d in range(4)]
        ada_landed = [sem(f"ada_landed{b}") for b in range(5)]
        ada_step = sem("ada_step")
        ada_read = sem("ada_read")
        dve_step = sem("dve_step")
        pool_step = sem("pool_step")
        squares = sem("squares")
        squares_summed = sem("squares_summed")
        dev_ready = sem("dev_ready")
        rstd_ready = sem("rstd_ready")
        scaled = sem("scaled")
        h_ready = sem("h_ready")
        x_ready = sem("x_ready")
        mix_high = sem("mix_high")
        mix_split = sem("mix_split")
        x_stored = sem("x_stored")
        x_back = sem("x_back")
        k_ready = sem("k_ready")
        pad_ready = sem("pad_ready")
        bias_ready = sem("bias_ready")
        scores_ready = sem("scores_ready")
        scores_read = sem("scores_read")
        max_ready = sem("max_ready")
        sink_ready = sem("sink_ready")
        exp_ready = sem("exp_ready")
        p_ready = sem("p_ready")
        pt_ready = sem("pt_ready")
        pt_read = sem("pt_read")
        o_ready = sem("o_ready")
        o_read = sem("o_read")
        log_ready = sem("log_ready")
        lse_ready = sem("lse_ready")
        log_diff = sem("log_diff")
        share_exp = sem("share_exp")
        share_ready = sem("share_ready")
        mixed = sem("mixed")
        hid_ready = sem("hid_ready")
        hid_high_ready = sem("hid_high_ready")
        hid_split = sem("hid_split")
        shifted = sem("shifted")
        w_high_ready = [sem(f"w_high_ready{s}") for s in range(3)]
        w_split = [sem(f"w_split{s}") for s in range(3)]
        ssm_landed = sem("ssm_landed")
        ssm_power = sem("ssm_power")
        ssm_exp = sem("ssm_exp")
        den_ready = sem("den_ready")
        inv_ready = sem("inv_ready")
        c_ready = sem("c_ready")
        powers_ready = sem("powers_ready")
        lag_ready = sem("lag_ready")
        lag_landed = sem("lag_landed")
        conv_tap = sem("conv_tap")
        conv_ready = sem("conv_ready")
        s_ready = sem("s_ready")
        glu_ready = sem("glu_ready")
        stored = sem("stored")

        block = ctx.enter_context(nc.Block())

        win_rows = [ffn_w_in[l].rearrange("(k p) n -> p k n", p=P) for l in range(2)]
        wout_rows = [ffn_w_out[l].rearrange("(f p) n -> p f n", p=P) for l in range(2)]
        mix_rows = [a_w_in[0].rearrange("(k p) n -> p k n", p=P), b_w_in[0].rearrange("(k p) n -> p k n", p=P)]
        wo_rows = [a_w_out[0].rearrange("(k p) n -> p k n", p=P), b_w_out[0].rearrange("(k p) n -> p k n", p=P)]
        ada_rows = [ada_w[l].rearrange("(k p) n -> p k n", p=P) for l in range(2)]
        in2_rows = w_in_2[0].rearrange("(k p) n -> p k n", p=P)
        glu_rows = w_glu_2[0].rearrange("(k p) n -> p k n", p=P)
        out2_rows = w_out_2[0].rearrange("(k p) n -> p k n", p=P)

        def mix_columns(u):
            a = UNITS[u]
            if a.layer == 0:
                return 256 * a.head, 1024 + DH * a.head, 1280 + DH * a.head
            g = 2 * a.group + a.head
            return 256 * g, 1536 + DH * g, 1920 + DH * g

        def acc_number(name):
            if name[0] == "ffn":
                used, _ = ACC[name[:2]]
                return name[2] % 3, used[name[2] % 3] + name[2] // 3 + 1
            return ACC[name][:2]

        def mix_weights(what, u):
            if what == "q":
                return wpair[0][:, :], w_low[2][:, :], w_low[0][:, :], 2 * (u - 4) + 1
            return wpair[1][:, 0:1024], w_low[1][:, 1024:2048], w_low[1][:, 0:1024], 2 * (u - 4) + 2

        def as_f32(ap):
            return ap.bitcast(F32)

        def v_free(u):
            return ACC[("v", u)][2] + 1

        def by_dilation(ap, dil):
            return ap.rearrange("p (a r) -> p r a", r=dil)

        def in_sequence(ap, dil):
            return ap.rearrange("p (r a) -> p r a", r=dil)

        @block.sync
        def _(sp):
            def into(name):
                s, last, _ = WTS[name]
                if last:
                    d, number = acc_number(last)
                    sp.wait_ge(acc_ready[d], number)
                return wpair[s], w_landed[s]

            def load(name, rows, k):
                w, landed = into(name)
                sp.dma_start(w[:, :].rearrange("p (k n) -> p k n", k=k), rows).then_inc(landed, 16)

            def load_mix(u):
                cq, ck, cv = mix_columns(u)
                rows = mix_rows[UNITS[u].layer]
                load(("q", u), rows[:, :, cq:cq + 256], KC)
                w, landed = into(("kv", u))
                kv = w[:, 0:1024].rearrange("p (k n) -> p k n", k=KC)
                sp.dma_start(kv[:, :, 0:DH], rows[:, :, ck:ck + DH]).then_inc(landed, 16)
                sp.dma_start(kv[:, :, DH:P], rows[:, :, cv:cv + DH]).then_inc(landed, 16)

            def load_ffn(l):
                lasts, _ = WTS[("ffn", l)]
                used, _ = ACC[("ffn", l)]
                hid_before = 2 * NF * l

                def group(g, s, rows=False):
                    if s == 2 or rows:
                        src, k = wout_rows[l][:, bass.ds(2 * g, 2), :], 2
                    else:
                        src, k = win_rows[l][:, :, bass.ds(256 * g + s * FF, 256)], KC
                    sp.dma_start(wpair[s][:, :].rearrange("p (k n) -> p k n", k=k), src).then_inc(w_landed[s], 16)

                for s in range(2):
                    d, number = acc_number(lasts[s])
                    sp.wait_ge(acc_ready[d], number)
                    group(0, s)
                sp.wait_ge(acc_ready[1], used[1] + 1)
                with sp.Fori(0, NF // 2) as i:
                    for b in range(2):
                        sp.wait_ge(acc_ready[2], 8 * i + (used[2] + 4 * b - 2))
                        group(2 * i + (b + 1), 0)
                        sp.wait_ge(hid_ready, hid_before + 4 * i + (2 * b + 2))
                        group(2 * i + (b + 1), 1)
                        sp.wait_ge(acc_ready[0], used[0] + 8 * i + (2 + 4 * b))
                        group(2 * i + b, 2)
                d, number = acc_number(("ffn", l, gate_up_at(NF - 1) + 1))
                sp.wait_ge(acc_ready[d], number)
                group(NF - 1, 0, True)

            for n, (ap, r) in enumerate(((ada_b.rearrange("l (m f) -> (l m) f", f=P), 96), (c.rearrange("o (m f) -> (o m) f", f=P), 8))):
                sp.dma_start(rows_in[96 * n:96 * n + r, 0, :], ap).then_inc(cond_landed, 16)
            sp.dma_start(hT[:, :, :], x[0].rearrange("(t p) d -> p t d", p=P)).then_inc(x_landed, 16)
            at = 0
            for ap in (norm_mix[0:1], norm_ffn[0:1], norm_mix[1:2], norm_ffn[1:2]):
                sp.dma_start(rows_in[at:at + 8, 1, :], ap.rearrange("o (m f) -> (o m) f", f=P)).then_inc(small_landed, 16)
                at += 8
            for ap in (final_norm, norm_gain_2[0], final_norm_gain_2):
                sp.dma_start(rows_in[at:at + 8, 1, :], ap.rearrange("(m f) -> m f", f=P)).then_inc(small_landed, 16)
                at += 8
            sp.dma_start(rows_in[56:60, 1, :], b_glu_2[0].rearrange("(m f) -> m f", f=P)).then_inc(small_landed, 16)
            sp.dma_start(rows_in[60:72, 1, :], conv_w_2[0].rearrange("k (m f) -> (k m) f", f=P)).then_inc(small_landed, 16)
            sp.dma_start(sink[:, :], a_sink.to_broadcast([P, 16])).then_inc(small_landed, 16)
            for u in range(4):
                load_mix(u)
            sp.wait_ge(ada_read, 20)
            for n in range(4):
                load(("wo", 0, n), wo_rows[0][:, :, 256 * n:256 * n + 256], KC)
            load_ffn(0)
            load_mix(4)
            used, freed = ACC[("ffn", 0)]
            for k in range(KC):
                pos = down_at(NF - 1) + k
                sp.wait_ge(acc_free[pos % 3], freed[pos % 3] + freed_at(pos) + 1)
                sp.dma_start(x_kept[:, k, :], xT[:, k, :]).then_inc(x_stored, 16)
            for u in range(5, 10):
                load_mix(u)
            d, number = acc_number(("kv", 9))
            sp.wait_ge(acc_ready[d], number)
            sp.wait_ge(x_stored, 16 * KC)
            sp.dma_start(xT[:, :, :], x_kept).then_inc(x_back, 16)
            for n in range(2):
                load(("wo", 1, n), wo_rows[1][:, :, 512 * n:512 * n + 512], 4)
            load_ffn(1)
            for j in range(4):
                for h, (first, second) in enumerate(((2, 4), (3, 5))):
                    w, landed = into(("conv", j, h))
                    two = w[:, :].rearrange("p (o k n) -> p o k n", o=2, k=KC)
                    for o, part in enumerate((first, second)):
                        at = SW * part + P * j
                        sp.dma_start(two[:, o], in2_rows[:, :, at:at + P]).then_inc(landed, 16)
            for n in range(2):
                load(("z", n), in2_rows[:, :, SW + 256 * n:SW + 256 * n + 256], KC)
            for n in range(2):
                load(("u", n), in2_rows[:, 4 * n:4 * n + 4, 0:SW], 4)
            load(("glu",), glu_rows, 4)
            for n in range(4):
                load(("out", n), out2_rows[:, :, 256 * n:256 * n + 256], KC)
            for t in range(ST):
                sp.wait_ge(acc_free[t % 3], ACC[("store", t)][2] + 1)
                sp.dma_start(out[0, P * t:P * t + P, :], arena[:, 1024 * t:1024 * t + 1024]).then_inc(stored, 16)
            sp.wait_ge(stored, 16 * ST)

        @block.gpsimd
        def _(pool):
            steps = [0]

            def after(ins):
                steps[0] += 1
                ins.then_inc(pool_step, 1)
                pool.wait_ge(pool_step, steps[0])

            after(nc.gpsimd.memset(ident[:, :], 0.0))
            nc.gpsimd.affine_select(out=ident[:, :], in_=ident[:, :], compare_op=ALU.not_equal, fill=1.0, base=0,
                                    pattern=[[-1, P]], channel_multiplier=1).then_inc(const_ready, 1)
            nc.gpsimd.memset(ones[:, :], 1.0).then_inc(const_ready, 1)

            def ada_load(l, first, n, dst, b):
                pool.dma_start(dst, ada_rows[l][:, :, bass.ds(first, n)]).then_inc(ada_landed[b], 16)

            for m in range(4):
                ada_load(0, 512 * m, 512, ada_start[:, m], m)

            after(nc.gpsimd.memset(pick[:, :, :], 1.0))
            after(nc.gpsimd.affine_select(out=pick[:, :, :], in_=pick[:, :, :], compare_op=ALU.is_ge, fill=0.0, base=0,
                                          pattern=[[P, 4], [1, P]], channel_multiplier=-DH))
            nc.gpsimd.affine_select(out=pick[:, :, :], in_=pick[:, :, :], compare_op=ALU.is_ge, fill=0.0, base=DH - 1,
                                    pattern=[[-P, 4], [-1, P]], channel_multiplier=DH).then_inc(const_ready, 1)

            def distances(dist, spare, first, reach):
                w = dist.shape[-1]
                after(nc.gpsimd.iota(dist, pattern=[[1, w]], base=first, channel_multiplier=-1, allow_small_or_imprecise_dtypes=True))
                after(nc.gpsimd.iota(spare, pattern=[[-1, w]], base=-first, channel_multiplier=1, allow_small_or_imprecise_dtypes=True))
                after(nc.gpsimd.affine_select(out=dist, in_=dist, compare_op=ALU.is_ge, fill=0.0, base=first, pattern=[[1, w]], channel_multiplier=-1))
                after(nc.gpsimd.affine_select(out=spare, in_=spare, compare_op=ALU.is_ge, fill=0.0, base=-first, pattern=[[-1, w]], channel_multiplier=1))
                after(nc.gpsimd.tensor_tensor(dist, dist, spare, ALU.add))
                if reach:
                    after(nc.gpsimd.affine_select(out=dist, in_=dist, compare_op=ALU.is_ge, fill=FAR, base=first + reach,
                                                  pattern=[[1, w]], channel_multiplier=-1))
                    after(nc.gpsimd.affine_select(out=dist, in_=dist, compare_op=ALU.is_ge, fill=FAR, base=reach - first,
                                                  pattern=[[-1, w]], channel_multiplier=1))

            def bias_tables(u):
                a = UNITS[u]
                lay = LAY[a.layer]
                w = P * a.chunks
                src = lay["dist16"] if a.dil == 16 else lay["dist"]
                if u % 4 >= 2 or u >= 6:
                    pool.wait_ge(scores_read, 32 * (u - 1))
                for h in range(4):
                    nc.gpsimd.tensor_scalar(lay["bias"][:, u % 2, h, 0:w], src[:, 0:w], -a.slope[h], None, ALU.mult).then_inc(bias_ready, 1)

            distances(LAY[0]["dist"], LAY[0]["bias"][:, 0, 0, :], -P, P)
            bias_tables(0)
            bias_tables(1)
            for u in range(4):
                if u >= 1 and u + 1 < 4:
                    bias_tables(u + 1)
                for k in range(4):
                    m = 4 * u + k
                    if m:
                        pool.wait_ge(ada_read, 4 + m)
                    ada_load(0, 2048 + 256 * m, 256, ada_mid, 4)

            pool.wait_ge(o_read, 64)
            pool.wait_ge(acc_free[0], ACC[("ada", 5)][2] + 1)

            def ada_rows_load(r, k):
                b = k % 2
                pool.dma_start(ada_ffn[:, b], ada_w[1, P * k:P * k + P, bass.ds(1024 * r, 1024)]).then_inc(ada_landed[b], 16)

            for k in range(KC):
                if k >= 2:
                    pool.wait_ge(ada_read, 19 + k)
                ada_rows_load(0, k)
            with pool.Fori(0, NF // 2) as i:
                for k in range(KC):
                    pool.wait_ge(ada_read, 8 * i + (27 + k))
                    ada_rows_load(i + 1, k)

            used, _ = ACC[("ffn", 0)]
            pool.wait_ge(acc_ready[3], used[3] + 5)
            lay = LAY[1]
            distances(lay["dist"], lay["bias"][:, 0, 0, :], -64, 64)
            distances(lay["dist16"], lay["bias"][:, 0, 0, 0:P], 0, 0)
            half = S // 16
            after(nc.gpsimd.affine_select(out=lay["dist16"][0:half, :], in_=lay["dist16"][0:half, :], compare_op=ALU.is_ge, fill=FAR,
                                          base=half - 1, pattern=[[-1, P]], channel_multiplier=0))
            after(nc.gpsimd.affine_select(out=lay["dist16"][half:P, :], in_=lay["dist16"][half:P, :], compare_op=ALU.is_ge, fill=FAR,
                                          base=-half, pattern=[[1, P]], channel_multiplier=0))
            nc.gpsimd.memset(lay["vT"][0:DH, 0:64], 0.0).then_inc(pad_ready, 1)
            nc.gpsimd.memset(lay["vT"][0:DH, 64 + S:P + S], 0.0).then_inc(pad_ready, 1)
            for u in range(4, 10):
                bias_tables(u)

            d, number = acc_number(("ffn", 1, down_at(NF - 1) + KC - 1))
            pool.wait_ge(acc_ready[d], number)
            for q in range(2):
                rows, groups = slice(NS * q, NS * q + NS), slice(NP * q, NP * q + NP)
                pool.dma_start(are[rows, :], ssm_a_re_2[0, groups].rearrange("c s -> s c"), allow_slow_non_contiguous=True).then_inc(ssm_landed, 16)
                pool.dma_start(aim[rows, :], ssm_a_im_2[0, groups].rearrange("c s -> s c"), allow_slow_non_contiguous=True).then_inc(ssm_landed, 16)
                pool.dma_start(ldt[rows, :], ssm_log_dt_2[:, groups].to_broadcast([NS, NP])).then_inc(ssm_landed, 16)
            pool.dma_start(d_in[0:GC, :], ssm_d_2[0].rearrange("g h -> h g"), allow_slow_non_contiguous=True).then_inc(ssm_landed, 16)
            for r, (b_ap, c_ap) in enumerate(((ssm_b_re_2, ssm_c_re_2), (ssm_b_im_2, ssm_c_im_2))):
                for q in range(2):
                    rows = slice(NS * q, NS * q + NS)
                    pool.dma_start(b_raw[rows, r], b_ap[0, NP * q:NP * q + NP].rearrange("c s h -> s c h")).then_inc(ssm_landed, 16)
                    for n in range(2):
                        eight = c_ap[0, NP * q + 8 * n:NP * q + 8 * n + 8]
                        pool.dma_start(c_raw[:, r, n, rows], eight.rearrange("c h s -> (c h) s")).then_inc(ssm_landed, 16)

            def ts(dst, a, s1, op0, s2=None, op1=None):
                after(nc.gpsimd.tensor_scalar(dst, a, s1, s2, op0, op1) if op1 else nc.gpsimd.tensor_scalar(dst, a, s1, None, op0))

            def tt(dst, a, b, op):
                after(nc.gpsimd.tensor_tensor(dst, a, b, op))

            def series(dst, z, coefficients):
                ts(dst, z, coefficients[0], ALU.mult)
                for v in coefficients[1:]:
                    ts(dst, dst, v, ALU.add)
                    tt(dst, dst, z, ALU.mult)

            def square(dst_re, dst_im, re, im):
                nc.gpsimd.tensor_tensor(st0, re, re, ALU.mult)
                nc.gpsimd.tensor_tensor(st1, im, im, ALU.mult)
                after(nc.gpsimd.tensor_tensor(st2, re, im, ALU.mult))
                nc.gpsimd.tensor_tensor(dst_re, st0, st1, ALU.subtract)
                after(nc.gpsimd.tensor_scalar(dst_im, st2, 2.0, None, ALU.mult))

            pool.wait_ge(ssm_landed, 16 * SSM_LOADS)
            tt(st0, are, are, ALU.mult)
            tt(st1, aim, aim, ALU.mult)
            nc.gpsimd.tensor_tensor(den, st0, st1, ALU.add).then_inc(den_ready, 1)
            pool.wait_ge(ssm_exp, 1)
            nc.gpsimd.tensor_tensor(st2, are, dt, ALU.mult).then_inc(ssm_power, 1)
            tt(angle, aim, dt, ALU.mult)
            ts(st0, angle, float(1 / (2 * np.pi)), ALU.mult, ROUND, ALU.add)
            ts(st0, st0, -ROUND, ALU.add)
            for part in TURN_PARTS:
                ts(st1, st0, -part, ALU.mult)
                tt(angle, angle, st1, ALU.add)
            ts(angle, angle, 0.25, ALU.mult)
            tt(st0, angle, angle, ALU.mult)
            series(z_im, st0, (1 / 362880, -1 / 5040, 1 / 120, -1 / 6))
            tt(z_im, z_im, angle, ALU.mult)
            tt(z_im, z_im, angle, ALU.add)
            series(z_re, st0, (-1 / 3628800, 1 / 40320, -1 / 720, 1 / 24, -0.5))
            for _ in range(2):
                tt(st0, z_im, z_re, ALU.mult)
                tt(st0, st0, z_im, ALU.add)
                tt(z_re, z_im, z_im, ALU.mult)
                ts(z_re, z_re, -2.0, ALU.mult)
                ts(z_im, st0, 2.0, ALU.mult)
            ts(z_re, z_re, 1.0, ALU.add)
            pool.wait_ge(ssm_exp, 2)
            tt(a_r, mag, z_re, ALU.mult)
            tt(a_i, mag, z_im, ALU.mult)
            ts(st3, a_r, -1.0, ALU.add)
            pool.wait_ge(inv_ready, 1)
            tt(st0, st3, are, ALU.mult)
            tt(st1, a_i, aim, ALU.mult)
            tt(st0, st0, st1, ALU.add)
            tt(in_r, st0, inv, ALU.mult)
            tt(st0, a_i, are, ALU.mult)
            tt(st1, st3, aim, ALU.mult)
            tt(st0, st0, st1, ALU.subtract)
            tt(in_i, st0, inv, ALU.mult)
            tt(mag8, mag, mag, ALU.mult)
            tt(mag8, mag8, mag8, ALU.mult)
            tt(mag8, mag8, mag8, ALU.mult)
            for _ in range(3):
                square(z_re, z_im, z_re, z_im)
            after(nc.gpsimd.tensor_copy(turn_r[:, 0:16], z_re))
            after(nc.gpsimd.tensor_copy(turn_i[:, 0:16], z_im))
            for n in range(1, 7):
                last, now = slice(16 * (n - 1), 16 * n), slice(16 * n, 16 * n + 16)
                square(turn_r[:, now], turn_i[:, now], turn_r[:, last], turn_i[:, last])

            def turns(ap, n):
                return ap.rearrange("p (c o) -> p c o", o=1).to_broadcast([P, NP, n])

            def cmul(out_re, out_im, xr, xi, yr, yi, minus=False):
                n = xr.shape[-1]
                t = [v[:, 0:NP * n].rearrange("p (c o) -> p c o", c=NP) for v in cm_tmp]
                nc.gpsimd.tensor_tensor(t[0], xr, yr, ALU.mult)
                nc.gpsimd.tensor_tensor(t[1], xi, yi, ALU.mult)
                nc.gpsimd.tensor_tensor(t[2], xr, yi, ALU.mult)
                after(nc.gpsimd.tensor_tensor(t[3], xi, yr, ALU.mult))
                nc.gpsimd.tensor_tensor(out_re, t[0], t[1], ALU.add if minus else ALU.subtract)
                after(nc.gpsimd.tensor_tensor(out_im, t[3], t[2], ALU.subtract if minus else ALU.add))

            cmul(bpow[:, 0, :, TB - 1, :], bpow[:, 1, :, TB - 1, :], b_raw[:, 0], b_raw[:, 1], turns(in_r, GC), turns(in_i, GC))
            for i in range(TB - 2, -1, -1):
                cmul(bpow[:, 0, :, i, :], bpow[:, 1, :, i, :], bpow[:, 0, :, i + 1, :], bpow[:, 1, :, i + 1, :], turns(a_r, GC), turns(a_i, GC))
            pool.wait_ge(c_ready, 1)
            pool.wait_ge(acc_free[3], ACC[("c^T",)][2] + 1)
            for j in range(TB):
                cmul(cpow[:, 0, :, j + 1, :], cpow[:, 1, :, j + 1, :], cpow[:, 0, :, j, :], cpow[:, 1, :, j, :], turns(a_r, GC), turns(a_i, GC), minus=True)
            nc.gpsimd.memset(phase[:, 0, :, 0:1], 1.0)
            after(nc.gpsimd.memset(phase[:, 1, :, 0:1], 0.0))
            for k in range(7):
                n = 2 ** k
                tr, ti = turn_r[:, 16 * k:16 * k + 16], turn_i[:, 16 * k:16 * k + 16]
                for at in range(0, n, 32):
                    m = min(32, n - at)
                    cmul(phase[:, 0, :, n + at:n + at + m], phase[:, 1, :, n + at:n + at + m],
                         phase[:, 0, :, at:at + m], phase[:, 1, :, at:at + m], turns(tr, m), turns(ti, m))
            nc.gpsimd.memset(lag_, 0.0).then_inc(powers_ready, 1)
            pool.wait_ge(powers_ready, 1)
            for half in range(2):
                pool.wait_ge(lag_ready, half + 1)
                for i in range(TB):
                    pool.dma_start(lag[GC * i:GC * i + GC, NP * half:NP * half + NP, GC * i:P],
                                   by_lag.rearrange("p g j h -> p g (j h)")[:, :, 0:P - GC * i]).then_inc(lag_landed, 16)

        @block.tensor
        def _(pe):
            def take(name):
                d, number, freed = ACC[name]
                if freed:
                    pe.wait_ge(acc_free[d], freed)
                return acc[d], acc_ready[d]

            def weights(name):
                s, _, landed = WTS[name]
                pe.wait_ge(w_landed[s], landed)
                return wpair[s]

            def dense(dst, chunks, w, src, first=True, last=True):
                for n, k in enumerate(chunks):
                    for t in range(2):
                        mm = nc.tensor.matmul(dst[:, HALF * t:HALF * t + HALF], w(k), src(k)[:, HALF * t:HALF * t + HALF],
                                              start=first and n == 0, stop=last and n == len(chunks) - 1)
                return mm

            def split_products(dst, chunks, high, low, src_high, src_low, wait=None, first=True, last=True):
                for n, k in enumerate(chunks):
                    if wait:
                        wait(k)
                    for w, srcs in ((high, (src_high, src_low)), (low, (src_high,))):
                        for m, src in enumerate(srcs):
                            for t in range(2):
                                mm = nc.tensor.matmul(dst[:, HALF * t:HALF * t + HALF], w(k), src(k)[:, HALF * t:HALF * t + HALF],
                                                      start=first and n == 0 and w is high and m == 0,
                                                      stop=last and n == len(chunks) - 1 and w is low)
                return mm

            def norm(n):
                dst, ready = take(("norm sum", n))
                pe.wait_ge(squares_summed, (KC - 1) * (n + 1))
                for t in range(ST):
                    mm = nc.tensor.matmul(dst[:, t:t + 1], hT[:, 0, P * t:P * t + P], ones[:, :], start=True, stop=True)
                mm.then_inc(ready, 1)
                dst, ready = take(("norm spread", n))
                pe.wait_ge(rstd_ready, n + 1)
                for t in range(ST):
                    mm = nc.tensor.matmul(dst[:, P * t:P * t + P], rst[:, n, 4, t:t + 1].to_broadcast([P, P]), ident[:, :], start=True, stop=True)
                mm.then_inc(ready, 1)

            def modulation(r, read):
                dst, ready = take(("ada", r))
                pe.wait_ge(ada_read, read)
                modulation_sums(dst, ada_acc).then_inc(ready, 1)

            def modulation_sums(dst, parts):
                for m in range(KC):
                    mm = nc.tensor.matmul(dst[:, m:m + 1], parts[:, P * m:P * m + P], ones[:, :], start=True, stop=True)
                return mm

            def project(u, part):
                lay = LAY[UNITS[u].layer]
                starts = (0, 4, 8, 11, 14, 16, 20, 24, 24)
                for what in range(3):
                    lo, hi = max(starts[part], KC * what) - KC * what, min(starts[part + 1], KC * what + KC) - KC * what
                    if lo >= hi:
                        continue
                    name = (("q0", "q1", "kv")[what], u)
                    if lo == 0:
                        take(name)
                    d = ACC[name][0]
                    first, last, chunks = lo == 0, hi == KC, range(lo, hi)
                    if u in (0, 4):
                        pe.wait_ge(h_ready, KC * 2 * UNITS[u].layer + hi)
                    at = P * what if what < 2 else 0
                    if u >= 4:
                        _, high, low, number = mix_weights("kv" if what == 2 else "q", u)
                        pe.wait_ge(mix_split, number)
                        high, low = (v.rearrange("p (k n) -> p k n", k=KC) for v in (high, low))
                        cols = slice(at, at + P)
                        mm = split_products(acc[d], chunks, lambda k: high[:, k, cols], lambda k: low[:, k, cols], lambda k: hT_high[:, k, :],
                                            lambda k: h_low_mix[:, k, :], None, first, last)
                    else:
                        w = weights(("kv" if what == 2 else "q", u))[:, :]
                        w = (w[:, 0:1024] if what == 2 else w).rearrange("p (k n) -> p k n", k=KC)
                        mm = dense(acc[d], chunks, lambda k: w[:, k, at:at + P], lambda k: hT[:, k, :], first, last)
                    if last:
                        mm.then_inc(acc_ready[d], 1)

            def turn_values(u):
                lay = LAY[UNITS[u].layer]
                dst, ready = take(("v", u))
                if u == 4:
                    pe.wait_ge(pad_ready, 2)
                for n in range(UNITS[u].vtiles):
                    mm = nc.tensor.transpose(dst[:, DH * n:DH * n + DH], lay["vT"][0:DH, P * n:P * n + P], ident[0:DH, 0:DH])
                mm.then_inc(ready, 1)

            def scores(t):
                u, n = t // 8, t % 8
                a, lay = UNITS[u], LAY[UNITS[u].layer]
                if n == 0:
                    pe.wait_ge(acc_free[0], ACC[("q1", u)][2] + 1)
                    pe.wait_ge(k_ready, 2 * (u + 1))
                lo, hi = a.window(n)
                key = P * n + a.first + a.pad
                for h in range(4):
                    e = 4 * t + h
                    if e >= 2:
                        pe.wait_ge(scores_read, e - 1)
                    rows = slice(DH * (h % 2), DH * (h % 2) + DH)
                    nc.tensor.matmul(acc[1][:, HALF * (e % 2) + lo:HALF * (e % 2) + hi], lay["q"][rows, u % 2, h // 2, P * n:P * n + P],
                                     lay["k"][rows, u % 2, key + lo:key + hi], start=True, stop=True).then_inc(scores_ready, 1)

            def turn(t):
                u, n = t // 8, t % 8
                lay = LAY[UNITS[u].layer]
                pe.wait_ge(p_ready, t + 1)
                if t:
                    pe.wait_ge(pt_read, t)
                for m, (c, _) in enumerate(UNITS[u].parts(n)):
                    for h in range(4):
                        mm = nc.tensor.transpose(psum[:, 2048 + HALF * m + P * h:2048 + HALF * m + P * h + P],
                                                 lay["s"][:, t % 2, h, P * c:P * c + P], ident[:, :])
                mm.then_inc(pt_ready, 1)

            def outputs(t):
                u, n = t // 8, t % 8
                lay = LAY[UNITS[u].layer]
                parts = UNITS[u].parts(n)
                if n == 0:
                    d, _, _ = ACC[("v", u)]
                    pe.wait_ge(acc_free[d], v_free(u))
                pe.wait_ge(pt_read, t + 1)
                if t:
                    pe.wait_ge(o_read, 2 * t)
                for m, (_, vt) in enumerate(parts):
                    mm = nc.tensor.matmul(psum[0:DH, 3584:4096], lay["v"][:, u % 2, vt, :], lay["pt"][:, t % 2, HALF * m:HALF * m + HALF],
                                          start=m == 0, stop=m == len(parts) - 1)
                mm.then_inc(o_ready, 1)

            def attention(first, last):
                for part in range(8):
                    project(first, part)
                turn_values(first)
                for t in range(8 * first, 8 * last + 2):
                    if t < 8 * last:
                        scores(t)
                    if t - 2 >= 8 * first:
                        outputs(t - 2)
                    if t // 8 + 1 < last:
                        project(t // 8 + 1, t % 8)
                    if 8 * first <= t - 1 < 8 * last:
                        turn(t - 1)
                    if t % 8 == 7 and t // 8 + 1 < last:
                        turn_values(t // 8 + 1)
                    if t % 8 == 7 and t < 32:
                        modulation(2 + t // 8, 4 + 4 * (t // 8 + 1))

            def ffn(l):
                used, freed = ACC[("ffn", l)]

                def at(pos, i):
                    d = pos % 3
                    pe.wait_ge(acc_free[d], TURN[d] * i + (freed[d] + freed_at(pos)))
                    return acc[d], acc_ready[d]

                def gate_up(pos, g, i, wait=None):
                    for n, (s, m) in enumerate(((0, 0), (0, 1), (1, 0), (1, 1))):
                        dst, ready = at(pos + n, i)
                        if m == 0:
                            pe.wait_ge(w_split[s], g + (LOADS[s] * l + 1))
                        low = w_low[s][:, :].rearrange("p (k n) -> p k n", k=KC)
                        high = w_high[:, s].rearrange("p (k n) -> p k n", k=KC)
                        cols = slice(P * m, P * m + P)
                        split_products(dst, range(KC), lambda k: high[:, k, cols], lambda k: low[:, k, cols], lambda k: hT_high[:, k, :],
                                       lambda k: h_low[:, k, :], wait if n == 0 else None).then_inc(ready, 1)

                def down(pos, g, b, i, last=False):
                    s = 0 if last else 2
                    pe.wait_ge(w_split[s], LOADS[0] * (l + 1) if last else g + (LOADS[2] * l + 1))
                    pe.wait_ge(hid_split, 2 * g + (2 * NF * l + 2))
                    low = w_low[s][:, :].rearrange("p (k n) -> p k n", k=2)
                    high = w_high[:, s].rearrange("p (k n) -> p k n", k=2)
                    for m in range(KC):
                        if not last and m in (0, 1):
                            pe.wait_ge(hid_ready, 2 * g + (2 * NF * l + 3 + m))
                        dst, ready = at(pos + m, i)
                        cols = slice(P * m, P * m + P)
                        split_products(dst, range(2), lambda k: high[:, k, cols], lambda k: low[:, k, cols], lambda k: hid_high[:, b, k, :],
                                       lambda k: hid_low[:, b, k, :]).then_inc(ready, 1)

                gate_up(0, 0, 0, lambda k: pe.wait_ge(h_ready, KC * (2 * l + 1) + k + 1))
                pe.wait_ge(hid_ready, 2 * NF * l + 2)
                with pe.Fori(0, NF // 2) as i:
                    for b in range(2):
                        gate_up(4 + 12 * b, 2 * i + (1 + b), i)
                        if l == 0 and b == 1:
                            pe.wait_ge(acc_free[3], i + freed[3])
                            pe.wait_ge(ada_read, 8 * i + 36)
                            modulation_sums(acc[3], ada_sum).then_inc(acc_ready[3], 1)
                        down(8 + 12 * b, 2 * i + b, b, i)
                down(down_at(NF - 1), NF - 1, 0, 0, True)

            pe.wait_ge(const_ready, 2)

            def vectors(n, r):
                dst, ready = take(("vectors", n))
                nc.tensor.transpose(dst[:, 0:r], rows_in[0:r, n, :], ident[0:r, 0:r]).then_inc(ready, 1)

            pe.wait_ge(cond_landed, 16 * 2)
            vectors(0, 104)
            pe.wait_ge(x_landed, 16)
            for k in range(KC):
                dst, ready = take(("x", k))
                for t in range(ST):
                    mm = nc.tensor.transpose(dst[:, P * t:P * t + P], hT[:, t, P * k:P * k + P], ident[:, :])
                mm.then_inc(ready, 1)
            norm(0)
            for r in range(2):
                modulation(r, 2 * r + 2)
            pe.wait_ge(small_landed, 16 * 10)
            vectors(1, 72)
            attention(0, 4)
            pe.wait_ge(o_read, 64)
            for m in range(KC):
                dst, ready = take(("wo", 0, m))
                w = weights(("wo", 0, m // 2))[:, :].rearrange("p (k n) -> p k n", k=KC)
                dense(dst, range(KC), lambda k: w[:, k, P * (m % 2):P * (m % 2) + P], lambda k: LAY[0]["oT"][:, k, :]).then_inc(ready, 1)
            dst, ready = take(("next ada",))
            pe.wait_ge(ada_read, 28)
            modulation_sums(dst, ada_sum).then_inc(ready, 1)
            norm(1)
            ffn(0)
            norm(2)
            attention(4, 10)
            pe.wait_ge(lse_ready, 3)
            for g in range(3):
                dst, ready = take(("lse", g))
                for n in range(ST):
                    mm = nc.tensor.transpose(dst[0:8, P * n:P * n + P], lse[:, g, n, :], ident[:, :])
                mm.then_inc(ready, 1)
            for m in range(4):
                for g in range(3):
                    dst, ready = take(("alpha", m, g))
                    pe.wait_ge(share_ready, 1)
                    pe.wait_ge(const_ready, 3)
                    for t in range(2):
                        mm = nc.tensor.matmul(dst[:, HALF * t:HALF * t + HALF], pick[:, m, :], lseT[:, g, HALF * t:HALF * t + HALF], start=True, stop=True)
                    mm.then_inc(ready, 1)
            for m in range(KC):
                dst, ready = take(("wo", 1, m))
                w = weights(("wo", 1, m // 4))[:, :].rearrange("p (k n) -> p k n", k=4)
                pe.wait_ge(mixed, 4)
                dense(dst, range(4), lambda k: w[:, k, P * (m % 4):P * (m % 4) + P], lambda k: LAY[1]["oT"][:, k, :]).then_inc(ready, 1)
            norm(3)
            ffn(1)

            norm(4)
            norm(5)
            pe.wait_ge(h_ready, 40)
            for j in range(4):
                for n in range(4):
                    dst, ready = take(("conv", j, n))
                    w = weights(("conv", j, n // 2))[:, :].rearrange("p (o k n) -> p o k n", o=2, k=KC)
                    dense(dst, range(KC), lambda k: w[:, n % 2, k, :], lambda k: hT[:, k, :]).then_inc(ready, 1)
                if j == 0:
                    dst, ready = take(("c^T",))
                    pe.wait_ge(ssm_landed, 16 * SSM_LOADS)
                    for r in range(2):
                        for n in range(2):
                            mm = nc.tensor.transpose(dst[:, 256 * r + P * n:256 * r + P * n + P], c_raw[:, r, n, :], ident[:, :])
                    mm.then_inc(ready, 1)
            pe.wait_ge(powers_ready, 1)
            for q in range(4):
                dst, ready = take(("win", q))
                for k in range(4):
                    for r in range(2):
                        at = P * (2 * k + r)
                        mm = nc.tensor.transpose(dst[:, at:at + P], bpow[:, r, 4 * q + k, :, :], ident[:, :])
                mm.then_inc(ready, 1)
            for d in range(4):
                dst, ready = take(("lag", d))
                for k in range(8):
                    g = 8 * d + k
                    q, cc = g // NP, g % NP
                    rows = slice(NS * q, NS * q + NS)
                    for r in range(2):
                        mm = nc.tensor.matmul(dst[0:GC, P * k:P * k + P], bpow[rows, r, cc, TB - 1, :], cpow[rows, r, cc, 0:TB, :],
                                              start=r == 0, stop=r == 1)
                mm.then_inc(ready, 1)
            for e in range(4):
                dst, ready = take(("z", e))
                w = weights(("z", e // 2))[:, :].rearrange("p (k n) -> p k n", k=KC)
                dense(dst, range(KC), lambda k: w[:, k, P * (e % 2):P * (e % 2) + P], lambda k: hT[:, k, :]).then_inc(ready, 1)
            w = [weights(("u", n))[:, :].rearrange("p (k n) -> p k n", k=4) for n in range(2)]
            for d in range(4):
                dst, ready = take(("u", d))
                for i in range(2):
                    for k in range(KC):
                        mm = nc.tensor.matmul(dst[:, HALF * i:HALF * i + HALF], hT[:, k, 2 * d + i::TB], w[k // 4][:, k % 4, :],
                                              start=k == 0, stop=k == KC - 1)
                mm.then_inc(ready, 1)
            for d in range(4):
                dst, ready = take(("u^T", d))
                pe.wait_ge(acc_free[d], ACC[("u", d)][2] + 1)
                if d == 0:
                    for dd in range(4):
                        pe.wait_ge(acc_free[dd], ACC[("u^T", dd)][2])
                for k in range(8):
                    g = 8 * d + k
                    mm = nc.tensor.transpose(dst[:, P * k:P * k + P], h_flat[:, P * g:P * g + P], ident[:, :])
                mm.then_inc(ready, 1)
            for h in range(2):
                for r, what in enumerate(("w re", "w im")):
                    dst, ready = take((what, h))
                    if h == 0 and r == 0:
                        for dd in range(4):
                            pe.wait_ge(acc_free[dd], ACC[("u^T", dd)][2] + 1)
                    for k in range(8):
                        cc = 8 * h + k
                        for q in range(2):
                            mm = nc.tensor.matmul(dst[NS * q:NS * q + NS, P * k:P * k + P], win[:, cc, r, NS * q:NS * q + NS],
                                                  uT[:, NP * q + cc, :], start=True, stop=True)
                    mm.then_inc(ready, 1)
            pe.wait_ge(lag_landed, 2 * 16 * TB)
            for d in range(4):
                dst, ready = take(("y", d))
                for k in range(8):
                    g = 8 * d + k
                    q, cc = g // NP, g % NP
                    rows = slice(NS * q, NS * q + NS)
                    nc.tensor.matmul(dst[:, P * k:P * k + P], uT[:, g, :], lag[:, g, :], start=True, stop=False)
                    if g == 0:
                        pe.wait_ge(s_ready, 4)
                    for r in range(2):
                        mm = nc.tensor.matmul(dst[:, P * k:P * k + P], s_prev[rows, r, cc, :], cpow[rows, r, cc, 1:TB + 1, :],
                                              start=False, stop=r == 1)
                mm.then_inc(ready, 1)
            for f in range(4):
                dst, ready = take(("y^T", f))
                if f == 0:
                    for dd in range(4):
                        pe.wait_ge(acc_free[dd], ACC[("y", dd)][2] + 1)
                for j in range(TB):
                    mm = nc.tensor.transpose(dst[:, P * j:P * j + P], y_blk[:, j, P * f:P * f + P], ident[:, :])
                mm.then_inc(ready, 1)
            w = weights(("glu",))[:, :].rearrange("p (k n) -> p k n", k=4)
            for e in range(4):
                dst, ready = take(("glu", e))
                if e == 0:
                    for dd in range(4):
                        pe.wait_ge(acc_free[dd], ACC[("y^T", dd)][2] + 1)
                dense(dst, range(4), lambda k: w[:, k, P * e:P * e + P], lambda k: yT[:, k, :]).then_inc(ready, 1)
            for m in range(KC):
                dst, ready = take(("out", m))
                w2 = weights(("out", m // 2))[:, :].rearrange("p (k n) -> p k n", k=KC)
                at = P * (m % 2)
                if m == 0:
                    pe.wait_ge(conv_ready, 4)
                dense(dst, range(4, 8), lambda k: w2[:, k, at:at + P], lambda k: y_conv[:, k - 4, :], True, False)
                if m == 0:
                    pe.wait_ge(glu_ready, 4)
                dense(dst, range(4), lambda k: w2[:, k, at:at + P], lambda k: y_ssm[:, k, :], False, True).then_inc(ready, 1)
            norm(6)
            pe.wait_ge(h_ready, 48)
            for t in range(ST):
                dst, ready = take(("store", t))
                for k in range(KC):
                    mm = nc.tensor.transpose(dst[:, P * k:P * k + P], hT[:, k, P * t:P * t + P], ident[:, :])
                mm.then_inc(ready, 1)

        @block.scalar
        def _(act):
            def ready(name):
                d, number = ACC[name][:2]
                act.wait_ge(acc_ready[d], number)
                return acc[d]

            def copied(name):
                d, _, freed = ACC[name]
                act.wait_ge(acc_free[d], freed + 1)

            def copy(dst, name, src=None, scale=1.0):
                a = ready(name)
                nc.scalar.activation(dst, a if src is None else src(a), ACT.Copy, scale=scale).then_inc(acc_free[ACC[name][0]], 1)

            def norm(n, wait_chunk):
                for k in range(KC):
                    wait_chunk(k)
                    nc.scalar.activation(hT[:, k, :], xT[:, k, :], ACT.Square).then_inc(squares, 1)
                if n in (1, 3):
                    first_weights(n // 2)
                if n == 2:
                    projection_high("q", 4)
                    projection_high("kv", 4)
                act.wait_ge(acc_free[3], ACC[("norm sum", n)][2] + 1)
                nc.scalar.activation(dev[:, n, :], var[:, n, :], ACT.Sqrt).then_inc(dev_ready, 1)
                if n < 4:
                    l, at = n // 2, 24 * (n % 2)
                    for k in range(KC):
                        act.wait_ge(scaled, KC * n + k + 1)
                        if n > 0:
                            whole = h_whole_mix if n == 2 else h_whole
                            nc.scalar.activation(hT_high[:, k, :], whole[:, k, :], ACT.Identity, bias=mod[:, l, at + k:at + k + 1]).then_inc(shifted, 1)
                            continue
                        nc.scalar.activation(hT[:, k, :], hT[:, k, :], ACT.Identity, bias=mod[:, l, at + k:at + k + 1]).then_inc(h_ready, 1)

            def projection_high(what, u):
                s, _, landed = WTS[(what, u)]
                whole, high, _, _ = mix_weights(what, u)
                act.wait_ge(w_landed[s], landed)
                nc.scalar.activation(high, whole, ACT.Copy).then_inc(mix_high, 1)

            def queries(u, m):
                a = UNITS[u]
                q = LAY[a.layer]["q"]
                copy(in_sequence(q[:, u % 2, m, :], a.dil), (f"q{m}", u), lambda s: by_dilation(s, a.dil), 1 / 8)

            def exponentials(t):
                u, n = t // 8, t % 8
                a, lay = UNITS[u], LAY[UNITS[u].layer]
                ti = t if a.layer == 0 else t - 32
                lo, hi = a.window(n)
                if a.layer == 0:
                    act.wait_ge(sink_ready, t + 1)
                    nc.scalar.activation(stat_s[:, t, 1, :], stat_s[:, t, 0, :], ACT.Exp)
                act.wait_ge(max_ready, t + 1)
                for h in range(4):
                    s = lay["s"][:, t % 2, h, lo:hi]
                    e = nc.scalar.activation(s, s, ACT.Exp, bias=stat_n[:, ti, h:h + 1], accum_out=stat_l[:, ti, h:h + 1])
                e.then_inc(exp_ready, 1)

            def turned_copy(t):
                u, n = t // 8, t % 8
                cols = HALF * len(UNITS[u].parts(n))
                act.wait_ge(pt_ready, t + 1)
                if t >= 2:
                    act.wait_ge(o_ready, t - 1)
                nc.scalar.activation(LAY[UNITS[u].layer]["pt"][:, t % 2, 0:cols], psum[:, 2048:2048 + cols], ACT.Copy).then_inc(pt_read, 1)

            def attention(first, last):
                queries(first, 0)
                queries(first, 1)
                if first == 4:
                    projection_high("q", 5)
                for t in range(8 * first, 8 * last + 1):
                    u, n = t // 8, t % 8
                    if u + 1 < last and n in (2, 5):
                        queries(u + 1, n // 3)
                    if u >= 4 and n == 2 and u + 1 < last:
                        projection_high("kv", u + 1)
                    if u >= 4 and n == 7 and u + 2 < last:
                        projection_high("q", u + 2)
                    if t < 8 * last:
                        exponentials(t)
                    if t > 8 * first:
                        turned_copy(t - 1)

            def ffn(l):
                used, freed = ACC[("ffn", l)]

                _, landed = WTS[("ffn", l)]

                def weights_high(s, g):
                    act.wait_ge(w_landed[s], 16 * g + 16 * (landed[s] + 1))
                    nc.scalar.activation(w_high[:, s], wpair[s][:, :], ACT.Copy).then_inc(w_high_ready[s], 1)

                def gates(pos, b, i, first=False):
                    for m in range(2):
                        at = pos + m
                        d = at % 3
                        if not first:
                            act.wait_ge(hid_ready, 4 * i + (2 * b + 2 * NF * l + m + 1))
                        act.wait_ge(acc_ready[d], 8 * i + (used[d] + at // 3 + 1))
                        nc.scalar.activation(gate_act[:, m, :], acc[d], ACT.Silu).then_inc(acc_free[d], 1)

                def hidden_high(b, g):
                    for m in range(2):
                        act.wait_ge(hid_ready, 2 * g + (2 * NF * l + m + 1))
                        nc.scalar.activation(hid_high[:, b, m, :], hid[:, b, m, :], ACT.Copy).then_inc(hid_high_ready, 1)

                def half(b, i, last=False):
                    weights_high(2, 2 * i + b)
                    gates(4 + 12 * b, b, i)
                    weights_high(0, NF if last else 2 * i + (b + 2))
                    hidden_high(1 - b, 2 * i + (b + 1))
                    if not last:
                        weights_high(1, 2 * i + (b + 2))

                gates(0, 0, 0, True)
                weights_high(0, 1)
                hidden_high(0, 0)
                weights_high(1, 1)
                with act.Fori(0, NF // 2 - 1) as i:
                    for b in range(2):
                        half(b, i)
                half(0, NF // 2 - 1)
                half(1, NF // 2 - 1, True)

            def first_weights(l):
                _, landed = WTS[("ffn", l)]
                d, number = acc_number(("wo", l, KC - 1))
                act.wait_ge(acc_ready[d], number)
                for s in range(2):
                    act.wait_ge(w_landed[s], 16 * (landed[s] + 1))
                    nc.scalar.activation(w_high[:, s], wpair[s][:, :], ACT.Copy).then_inc(w_high_ready[s], 1)

            def ffn_done(l, k):
                used, freed = ACC[("ffn", l)]
                pos = down_at(NF - 1) + k
                act.wait_ge(acc_free[pos % 3], freed[pos % 3] + freed_at(pos) + 1)

            copied(("vectors", 0))
            nc.scalar.activation(cond[:, :], vec[:, COND:COND + KC], ACT.Silu).then_inc(cond_ready, 1)
            for k in range(1, KC, 2):
                copy(xT[:, k, :], ("x", k))
            ready(("x", KC - 1))
            norm(0, lambda k: copied(("x", k)))
            attention(0, 4)
            norm(1, lambda k: copied(("wo", 0, k)))
            ffn(0)
            norm(2, lambda k: ffn_done(0, k))
            attention(4, 10)
            act.wait_ge(p_ready, 80)
            nc.scalar.activation(loglen[:, :, :, :].rearrange("p u n h -> p (u n h)"), stat_l[:, :, :].rearrange("p t h -> p (t h)"), ACT.Ln).then_inc(log_ready, 1)
            act.wait_ge(log_diff, 3)
            nc.scalar.activation(lseT, lseT, ACT.Exp).then_inc(share_exp, 1)
            norm(3, lambda k: copied(("wo", 1, k)))
            ffn(1)
            norm(4, lambda k: ffn_done(1, k))
            norm(5, lambda k: act.wait_ge(x_ready, k + 1))
            act.wait_ge(ssm_landed, 16 * SSM_LOADS)
            nc.scalar.activation(dt, ldt, ACT.Exp).then_inc(ssm_exp, 1)
            act.wait_ge(ssm_power, 1)
            nc.scalar.activation(mag, st2, ACT.Exp).then_inc(ssm_exp, 1)

            for j in range(4):
                if j:
                    act.wait_ge(conv_ready, j)
                copy(conv_y, ("conv", j, 0))
                copied(("conv", j, 1))
                nc.scalar.activation(conv_y, conv_v[:, 0:S], ACT.Copy, scale=vec[:, CONV_W + j:CONV_W + j + 1]).then_inc(conv_tap, 1)
                copied(("conv", j, 2))
                nc.scalar.activation(conv_v[:, 2:2 + S], ready(("conv", j, 3)), ACT.Silu).then_inc(acc_free[3], 1)
            for e in range(4):
                nc.scalar.activation(zs[:, e, :], ready(("z", e)), ACT.Silu).then_inc(acc_free[e], 1)
            ready(("u", 3))
            for d in (0, 2):
                copy(u_blk[:, 2 * d:2 * d + 2], ("u", d), lambda s: s.rearrange("p (i g h) -> p i g h", i=2, g=NG))
            for d in (0, 2):
                copy(uT[:, 8 * d:8 * d + 8, :].rearrange("p g b -> p (g b)"), ("u^T", d))
            for d in range(4):
                src = ready(("y", d)).rearrange("p (g j h) -> p j g h", g=8, j=TB)
                nc.scalar.activation(y_blk[:, :, P * d:P * d + P].rearrange("p j (g h) -> p j g h", g=8), src,
                                     ACT.Gelu_apprx_tanh).then_inc(acc_free[d], 1)
            for f in (0, 2):
                copy(yT[:, f, :].rearrange("p (b j) -> p j b", j=TB), ("y^T", f), lambda s: s.rearrange("p (j b) -> p j b", j=TB))
            for e in range(4):
                if e >= 2:
                    act.wait_ge(glu_ready, e - 1)
                nc.scalar.activation(tmp[e % 2], ready(("glu", e)), ACT.Sigmoid, bias=vec[:, B_GLU + e:B_GLU + e + 1]).then_inc(acc_free[e], 1)
            norm(6, lambda k: copied(("out", k)))
            for t in range(0, ST, 2):
                copy(arena[:, S * t:S * t + S], ("store", t))

        @block.vector
        def _(dve):
            steps = [0]

            def after(ins):
                steps[0] += 1
                ins.then_inc(dve_step, 1)
                dve.wait_ge(dve_step, steps[0])

            def ready(name):
                d, number = ACC[name][:2]
                dve.wait_ge(acc_ready[d], number)
                return acc[d]

            def copied(name):
                d, _, freed = ACC[name]
                dve.wait_ge(acc_free[d], freed + 1)

            def free(name):
                return acc_free[ACC[name][0]]

            def copy(dst, name, src=None):
                a = ready(name)
                nc.vector.tensor_copy(dst, a if src is None else src(a)).then_inc(free(name), 1)

            def piece(buf, dst, landed, value, step, read):
                dve.wait_ge(landed, value)
                nc.vector.tensor_scalar(dst, buf[:, 0, :], cond[:, 0:1], None, ALU.mult).then_inc(ada_step, 1)
                for k in range(1, KC):
                    dve.wait_ge(ada_step, step + k)
                    nc.vector.scalar_tensor_tensor(dst, buf[:, k, :], cond[:, k:k + 1], dst, ALU.mult, ALU.add).then_inc(
                        ada_step if k < KC - 1 else ada_read, 1)

            def modulation(r):
                name = ("ada", r)
                nc.vector.tensor_tensor(mod[:, 0, 8 * r:8 * r + 8], ready(name)[:, 0:8], vec[:, 8 * r:8 * r + 8], ALU.add).then_inc(free(name), 1)

            def sum_squares(n, k):
                if k > 0:
                    dve.wait_ge(squares, KC * n + k + 1)
                    if (KC - 1) * n + k > 1:
                        dve.wait_ge(squares_summed, (KC - 1) * n + k - 1)
                    nc.vector.tensor_tensor(hT[:, 0, :], hT[:, 0, :], hT[:, k, :], ALU.add).then_inc(squares_summed, 1)

            def norm(n):
                deviations(n)
                if n in (1, 3):
                    first_weights(n // 2)
                if n == 2:
                    projection_low("q", 4)
                    projection_low("kv", 4)
                normalise(n)

            def deviations(n):
                sum_squares(n, KC - 1)
                a = ready(("norm sum", n))
                nc.vector.tensor_scalar(var[:, n, :], a[:, 0:ST], 1.0 / D, EPS, ALU.mult, ALU.add).then_inc(acc_free[3], 1)
                dve.wait_ge(dev_ready, n + 1)
                r = [rst[:, n, i, :] for i in range(5)]
                after(nc.vector.reciprocal(r[0], dev[:, n, :]))
                after(nc.vector.tensor_tensor(r[1], r[0], r[0], ALU.mult))
                after(nc.vector.tensor_tensor(r[2], r[1], var[:, n, :], ALU.mult))
                after(nc.vector.tensor_scalar(r[3], r[2], -0.5, 1.5, ALU.mult, ALU.add))
                nc.vector.tensor_tensor(r[4], r[0], r[3], ALU.mult).then_inc(rstd_ready, 1)

            def normalise(n):
                g = vec[:, GAINS + 8 * n:GAINS + 8 * n + 8]
                if n < 4:
                    l, at = n // 2, 24 * (n % 2) + 8
                    after(nc.vector.scalar_tensor_tensor(gain[:, n, :], mod[:, l, at:at + 8], 1.0, g, ALU.add, ALU.mult))
                else:
                    after(nc.vector.tensor_copy(gain[:, n, :], g))
                spread = ready(("norm spread", n))

                def low(k):
                    dve.wait_ge(shifted, KC * (n - 1) + k + 1)
                    if n == 2:
                        dve.wait_ge(x_stored, 16 * KC)
                    at = 24 * (n % 2) + k
                    v, shift = (h_whole_mix if n == 2 else h_whole)[:, k, :], mod[:, n // 2, at:at + 1]
                    nc.vector.scalar_tensor_tensor((h_low_mix if n == 2 else h_low)[:, k, :], v, shift, as_f32(hT_high[:, k, :]), ALU.add, ALU.subtract).then_inc(h_ready, 1)

                for k in range(KC):
                    dst = xT if n == 4 else h_whole if n in (1, 3) else h_whole_mix if n == 2 else hT
                    done = scaled if n < 4 else x_ready if n == 4 else h_ready
                    nc.vector.scalar_tensor_tensor(dst[:, k, :], xT[:, k, :], gain[:, n, k:k + 1], spread, ALU.mult, ALU.mult).then_inc(done, 1)
                    if n == 4:
                        sum_squares(5, k - 1)
                    if n in (1, 2, 3) and k > 0:
                        low(k - 1)
                if n in (1, 2, 3):
                    low(KC - 1)

            def projection_low(what, u):
                whole, high, low, number = mix_weights(what, u)
                dve.wait_ge(mix_high, number)
                nc.vector.tensor_tensor(low, whole, as_f32(high), ALU.subtract).then_inc(mix_split, 1)

            def keys_values(u):
                a, lay = UNITS[u], LAY[UNITS[u].layer]
                src = ready(("kv", u))
                for half in range(2):
                    dst = lay["k"][DH * half:DH * half + DH, u % 2, a.pad:a.pad + S]
                    nc.vector.tensor_copy(in_sequence(dst, a.dil), by_dilation(src[0:DH], a.dil)).then_inc(k_ready, 1)
                nc.vector.tensor_copy(in_sequence(lay["vT"][0:DH, a.pad:a.pad + S], a.dil), by_dilation(src[DH:P], a.dil)).then_inc(acc_free[0], 1)

            def values(u):
                a = UNITS[u]
                copy(LAY[a.layer]["v"][:, u % 2, 0:a.vtiles, :].rearrange("p n d -> p (n d)"), ("v", u), lambda s: s[:, 0:DH * a.vtiles])

            def biased(t):
                u, n = t // 8, t % 8
                a, lay = UNITS[u], LAY[UNITS[u].layer]
                ti = t if a.layer == 0 else t - 32
                lo, hi = a.window(n)
                if n == 0:
                    dve.wait_ge(bias_ready, 4 * (u + 1))
                if t >= 2:
                    dve.wait_ge(pt_ready, t - 1)
                if a.layer == 1 and a.chunks == 2:
                    if lo > 0:
                        nc.vector.memset(lay["s"][:, t % 2, :, 0:lo], 0.0)
                    if hi < P * a.chunks:
                        nc.vector.memset(lay["s"][:, t % 2, :, hi:P * a.chunks], 0.0)
                for h in range(4):
                    e = 4 * t + h
                    at = S + HALF * (e % 2)
                    start = sink[:, 4 * a.head + h:4 * a.head + h + 1] if a.layer == 0 else LOWEST
                    dve.wait_ge(scores_ready, e + 1)
                    nc.vector.tensor_tensor_reduce(out=lay["s"][:, t % 2, h, lo:hi], in0=psum[:, at + lo:at + hi], in1=lay["bias"][:, u % 2, h, lo:hi],
                                                   scale=1.0, scalar=start, op0=ALU.add, op1=ALU.max,
                                                   accum_out=stat_m[:, ti, h:h + 1]).then_inc(scores_read, 1)
                dve.wait_ge(scores_read, 4 * t + 4)
                nc.vector.tensor_scalar(stat_n[:, ti, :], stat_m[:, ti, :], -1.0, None, ALU.mult).then_inc(max_ready, 1)
                if a.layer == 0:
                    dve.wait_ge(max_ready, t + 1)
                    nc.vector.tensor_tensor(stat_s[:, t, 0, :], sink[:, 4 * a.head:4 * a.head + 4], stat_n[:, t, :], ALU.add).then_inc(sink_ready, 1)

            def normalised(t):
                u, n = t // 8, t % 8
                a, lay = UNITS[u], LAY[UNITS[u].layer]
                ti = t if a.layer == 0 else t - 32
                lo, hi = a.window(n)
                dve.wait_ge(exp_ready, t + 1)
                total = stat_l[:, ti, :]
                if a.layer == 0:
                    total = stat_s[:, t, 2, :]
                    after(nc.vector.tensor_tensor(total, stat_l[:, t, :], stat_s[:, t, 1, :], ALU.add))
                after(nc.vector.reciprocal(stat_i[:, ti, :], total))
                for h in range(4):
                    s = lay["s"][:, t % 2, h, lo:hi]
                    ins = nc.vector.tensor_scalar(s, s, stat_i[:, ti, h:h + 1], None, ALU.mult)
                ins.then_inc(p_ready, 1)

            def outputs(t):
                u, n = t // 8, t % 8
                a, lay = UNITS[u], LAY[UNITS[u].layer]
                m = 4 * a.group + 2 * a.head if a.layer == 1 else 2 * a.head
                dve.wait_ge(o_ready, t + 1)
                src = psum[0:DH, 3584:4096].rearrange("p (m r q) -> p m r q", m=2, r=2)
                for half in range(2):
                    dst, rows = lay["oT"][DH * half:DH * half + DH, m:m + 2, :], src[:, :, half, :]
                    if a.dil == 1:
                        dst = dst[:, :, P * n:P * n + P]
                    elif a.dil == 4:
                        dst = dst.rearrange("p m (a r) -> p m r a", r=4)[:, :, n // 2, P * (n % 2):P * (n % 2) + P]
                    else:
                        dst = dst.rearrange("p m (a r) -> p m r a", r=16)[:, :, 2 * n:2 * n + 2, :]
                        rows = rows.rearrange("p m (r a) -> p m r a", r=2)
                    nc.vector.tensor_copy(dst, rows).then_inc(o_read, 1)

            def attention(first, last):
                keys_values(first)
                if first == 4:
                    projection_low("q", 5)
                for t in range(8 * first, 8 * last + 2):
                    u, n = t // 8, t % 8
                    if n == 0 and u < last:
                        values(u)
                        if 0 < u < 4:
                            modulation(1 + u)
                    if n == 7 and u + 1 < last:
                        keys_values(u + 1)
                    if t < 8 * last:
                        biased(t)
                    if 8 * first <= t - 1 < 8 * last:
                        normalised(t - 1)
                    if t - 2 >= 8 * first:
                        outputs(t - 2)
                    if u >= 4 and n == 2 and u + 1 < last:
                        projection_low("kv", u + 1)
                    if u >= 4 and n == 7 and u + 2 < last:
                        projection_low("q", u + 2)
                    if t < 32 and n % 2 == 0:
                        m = 4 * u + n // 2
                        piece(ada_mid, ada_acc[:, 128 * n:128 * n + 256], ada_landed[4], 16 * (m + 1), 7 * (4 + m), 4 + m)

            def add_product(name, k, g):
                a = ready(name)
                ins = nc.vector.scalar_tensor_tensor(xT[:, k, :], a, g, xT[:, k, :], ALU.mult, ALU.add)
                ins.then_inc(free(name), 1)

            def next_modulation(chunks, i):
                for k in chunks:
                    dve.wait_ge(ada_read, 8 * i + (28 + k))
                    dve.wait_ge(ada_landed[k % 2], 64 * i + (80 + 16 * (k // 2 + 1)))
                    if k == 0:
                        nc.vector.tensor_scalar(ada_sum, ada_ffn[:, 0], cond[:, 0:1], None, ALU.mult).then_inc(ada_read, 1)
                    else:
                        nc.vector.scalar_tensor_tensor(ada_sum, ada_ffn[:, k % 2], cond[:, k:k + 1], ada_sum, ALU.mult, ALU.add).then_inc(ada_read, 1)

            def ffn(l):
                used, freed = ACC[("ffn", l)]

                def weights_low(s, g):
                    dve.wait_ge(w_high_ready[s], g + (LOADS[s] * l + 1))
                    w = wpair[s][:, :]
                    nc.vector.tensor_tensor(w_low[s][:, :], w, as_f32(w_high[:, s]), ALU.subtract).then_inc(w_split[s], 1)

                def hidden(pos, b, i, g):
                    for m in range(2):
                        gate, up = pos + m, pos + 2 + m
                        dve.wait_ge(acc_free[gate % 3], TURN[gate % 3] * i + (freed[gate % 3] + freed_at(gate) + 1))
                        dve.wait_ge(acc_ready[up % 3], 8 * i + (used[up % 3] + up // 3 + 1))
                        nc.vector.tensor_tensor(hid[:, b, m, :], gate_act[:, m, :], acc[up % 3], ALU.mult).then_inc(hid_ready, 1)
                    for m in range(2):
                        dve.wait_ge(hid_high_ready, 2 * g + (2 * NF * l + m + 1))
                        v = hid[:, b, m, :]
                        nc.vector.tensor_tensor(hid_low[:, b, m, :], v, as_f32(hid_high[:, b, m, :]), ALU.subtract).then_inc(hid_split, 1)

                def down(pos, i, last=False):
                    for k in range(KC):
                        d, number = (pos + k) % 3, (pos + k) // 3
                        dve.wait_ge(acc_ready[d], 8 * i + (used[d] + number + 1))
                        nc.vector.scalar_tensor_tensor(xT[:, k, :], acc[d], mod[:, l, 40 + k:41 + k], xT[:, k, :], ALU.mult, ALU.add).then_inc(acc_free[d], 1)
                        if last:
                            sum_squares(2 * l + 2, k - 1)

                def modulation_sums(i):
                    dve.wait_ge(acc_ready[3], i + (used[3] + 1))
                    at = 8 * i + 8
                    nc.vector.tensor_tensor(mod[:, 1, bass.ds(at, 8)], acc[3][:, 0:8], vec[:, bass.ds(8 * i + 56, 8)], ALU.add).then_inc(acc_free[3], 1)

                def half(b, i, last=False):
                    weights_low(2, 2 * i + b)
                    if l == 0:
                        next_modulation(range(4 * b, 4 * b + 4), i)
                    hidden(4 + 12 * b, 1 - b, i, 2 * i + (b + 1))
                    if l == 0 and b == 1:
                        modulation_sums(i)
                    weights_low(0, NF if last else 2 * i + (b + 2))
                    down(8 + 12 * b, i)
                    if not last:
                        weights_low(1, 2 * i + (b + 2))

                hidden(0, 0, 0, 0)
                weights_low(0, 1)
                weights_low(1, 1)
                with dve.Fori(0, NF // 2 - 1) as i:
                    for b in range(2):
                        half(b, i)
                half(0, NF // 2 - 1)
                half(1, NF // 2 - 1, True)
                down(down_at(NF - 1), 0, True)

            def first_weights(l):
                for s in range(2):
                    dve.wait_ge(w_high_ready[s], LOADS[s] * l + 1)
                    w = wpair[s][:, :]
                    nc.vector.tensor_tensor(w_low[s][:, :], w, as_f32(w_high[:, s]), ALU.subtract).then_inc(w_split[s], 1)

            copy(vec[:, 0:104], ("vectors", 0), lambda s: s[:, 0:104])
            for k in range(0, KC, 2):
                copy(xT[:, k, :], ("x", k))
            for k in range(1, KC - 1):
                sum_squares(0, k)
            deviations(0)
            dve.wait_ge(cond_ready, 1)
            for m in range(4):
                piece(ada_start[:, m], ada_acc[:, HALF * (m % 2):HALF * (m % 2) + HALF], ada_landed[m], 16, 7 * m, m)
                if m % 2:
                    modulation(m // 2)
            for k in range(1, KC, 2):
                copied(("x", k))
            copy(vec[:, 104:176], ("vectors", 1), lambda s: s[:, 0:72])
            copied(("vectors", 1))
            normalise(0)
            dve.wait_ge(small_landed, 16 * 10)
            attention(0, 4)
            modulation(5)
            next_modulation(range(KC), -1)
            for k in range(KC):
                add_product(("wo", 0, k), k, mod[:, 0, 16 + k:17 + k])
                sum_squares(1, k - 1)
            name = ("next ada",)
            nc.vector.tensor_tensor(mod[:, 1, 0:8], ready(name)[:, 0:8], vec[:, 48:56], ALU.add).then_inc(free(name), 1)
            norm(1)
            ffn(0)
            norm(2)
            attention(4, 10)
            dve.wait_ge(log_ready, 1)
            for g in range(3):
                nc.vector.tensor_tensor(lse[:, g].rearrange("p n (j h) -> p j n h", j=2), loglen[:, 2 * g:2 * g + 2],
                                        stat_n[:, 16 * g:16 * g + 16, :].rearrange("p (j n) h -> p j n h", j=2), ALU.subtract).then_inc(lse_ready, 1)
            for g, dil in enumerate((1, 4, 16)):
                copy(by_dilation(lseT[:, g], dil), ("lse", g), lambda s: in_sequence(s[0:8], dil))
            for g in range(3):
                copied(("lse", g))
            after(nc.vector.tensor_tensor(top, lseT[:, 0], lseT[:, 1], ALU.max))
            after(nc.vector.tensor_tensor(top, top, lseT[:, 2], ALU.max))
            for g in range(3):
                nc.vector.tensor_tensor(lseT[:, g], lseT[:, g], top, ALU.subtract).then_inc(log_diff, 1)
            dve.wait_ge(share_exp, 1)
            after(nc.vector.tensor_tensor(esum, lseT[:, 0], lseT[:, 1], ALU.add))
            after(nc.vector.tensor_tensor(esum, esum, lseT[:, 2], ALU.add))
            after(nc.vector.reciprocal(esum, esum))
            for g in range(3):
                ins = nc.vector.tensor_tensor(lseT[:, g], lseT[:, g], esum, ALU.mult)
            ins.then_inc(share_ready, 1)
            for m in range(4):
                for g in range(3):
                    name = ("alpha", m, g)
                    nc.vector.tensor_tensor(mix_tmp[:, g], LAY[1]["oT"][:, 4 * g + m, :], ready(name), ALU.mult).then_inc(free(name), 1)
                copied(("alpha", m, 2))
                after(nc.vector.tensor_tensor(mix_tmp[:, 3], mix_tmp[:, 0], mix_tmp[:, 1], ALU.add))
                nc.vector.tensor_tensor(LAY[1]["oT"][:, m, :], mix_tmp[:, 3], mix_tmp[:, 2], ALU.add).then_inc(mixed, 1)
                dve.wait_ge(mixed, m + 1)
            dve.wait_ge(x_back, 16)
            for k in range(KC):
                add_product(("wo", 1, k), k, mod[:, 1, 16 + k:17 + k])
                sum_squares(3, k - 1)
            norm(3)
            ffn(1)

            norm(4)
            dve.wait_ge(x_ready, KC)
            norm(5)
            dve.wait_ge(den_ready, 1)
            nc.vector.reciprocal(inv, den).then_inc(inv_ready, 1)

            after(nc.vector.memset(conv_v[:, 0:2], 0.0))
            for j in range(4):
                def tap(k):
                    at = CONV_W + 4 * k + j
                    return vec[:, at:at + 1]

                copied(("conv", j, 0))
                nc.vector.tensor_tensor(conv_v[:, 2:2 + S], conv_y, ready(("conv", j, 1)), ALU.mult).then_inc(acc_free[1], 1)
                dve.wait_ge(conv_tap, j + 1)
                after(nc.vector.scalar_tensor_tensor(conv_y, conv_v[:, 1:1 + S], tap(1), conv_y, ALU.mult, ALU.add))
                after(nc.vector.scalar_tensor_tensor(conv_y, conv_v[:, 2:2 + S], tap(2), conv_y, ALU.mult, ALU.add))
                nc.vector.tensor_tensor(conv_y, conv_y, ready(("conv", j, 2)), ALU.mult).then_inc(acc_free[2], 1)
                copied(("conv", j, 3))
                nc.vector.tensor_tensor(y_conv[:, j, :], conv_y, conv_v[:, 2:2 + S], ALU.mult).then_inc(conv_ready, 1)
                if j == 0:
                    c_rows = ready(("c^T",))[:, 0:512].rearrange("p (r c h) -> p r c h", r=2, c=NP)
                    nc.vector.tensor_copy(cpow[:, 0, :, 0, :], c_rows[:, 0]).then_inc(c_ready, 1)
                    nc.vector.tensor_scalar(cpow[:, 1, :, 0, :], c_rows[:, 1], -1.0, None, ALU.mult).then_inc(acc_free[3], 1)
            for q in range(4):
                copy(win[:, 4 * q:4 * q + 4].rearrange("p c r s -> p (c r s)"), ("win", q))
            dve.wait_ge(conv_ready, 4)
            for half in range(2):
                if half:
                    dve.wait_ge(lag_landed, 16 * TB)
                for d in range(2):
                    copy(by_lag[:, 8 * d:8 * d + 8].rearrange("p g j h -> p (g j h)"), ("lag", 2 * half + d), lambda s: s[0:GC])
                copied(("lag", 2 * half + 1))
                for g in range(NP):
                    v, n = by_lag[:, g, 0, :], NP * half + g
                    ins = nc.vector.scalar_tensor_tensor(v, ident[0:GC, 0:GC], d_in[0:GC, n:n + 1], v, ALU.mult, ALU.add)
                ins.then_inc(lag_ready, 1)
            ready(("u", 3))
            for d in (1, 3):
                copy(u_blk[:, 2 * d:2 * d + 2], ("u", d), lambda s: s.rearrange("p (i g h) -> p i g h", i=2, g=NG))
            for d in (1, 3):
                copy(uT[:, 8 * d:8 * d + 8, :].rearrange("p g b -> p (g b)"), ("u^T", d))

            def full(ap):
                return ap.rearrange("p (c b) -> p c b", b=NB)

            dve.wait_ge(lag_landed, 2 * 16 * TB)
            for h in range(2):
                c8 = slice(8 * h, 8 * h + 8)
                wr, wi = full(ready(("w re", h))), full(ready(("w im", h)))
                pc, ps = phase[:, 0, c8, :], phase[:, 1, c8, :]
                t0, t1 = full(tmp[0]), full(tmp[1])
                nc.vector.tensor_tensor(t0, wr, pc, ALU.mult)
                after(nc.vector.tensor_tensor(t1, wi, ps, ALU.mult))
                after(nc.vector.tensor_tensor(turned[:, 0, c8, :], t0, t1, ALU.add))
                nc.vector.tensor_tensor(t0, wr, ps, ALU.mult).then_inc(free(("w re", h)), 1)
                nc.vector.tensor_tensor(t1, wi, pc, ALU.mult).then_inc(free(("w im", h)), 1)
                copied(("w im", h))
                after(nc.vector.tensor_tensor(turned[:, 1, c8, :], t1, t0, ALU.subtract))
            for cc in range(NP):
                for r in range(2):
                    z = turned[:, r, cc, :]
                    ins = nc.vector.tensor_tensor_scan(z, mag8[:, cc:cc + 1].to_broadcast([P, NB]), z, 0.0, ALU.mult, ALU.add)
            after(ins)
            for r in range(2):
                ins = nc.vector.memset(s_prev[:, r, :, 0:1], 0.0)
            for h in range(2):
                c8 = slice(8 * h, 8 * h + 8)
                zr, zi = turned[:, 0, c8, 0:NB - 1], turned[:, 1, c8, 0:NB - 1]
                pc, ps = phase[:, 0, c8, 0:NB - 1], phase[:, 1, c8, 0:NB - 1]
                t0, t1 = full(tmp[0])[:, :, 0:NB - 1], full(tmp[1])[:, :, 0:NB - 1]
                for r, (p0, p1, op) in enumerate(((pc, ps, ALU.subtract), (ps, pc, ALU.add))):
                    nc.vector.tensor_tensor(t0, zr, p0, ALU.mult)
                    after(nc.vector.tensor_tensor(t1, zi, p1, ALU.mult))
                    nc.vector.tensor_tensor(s_prev[:, r, c8, 1:NB], t0, t1, op).then_inc(s_ready, 1)
                    dve.wait_ge(s_ready, 2 * h + r + 1)
            for f in (1, 3):
                copy(yT[:, f, :].rearrange("p (b j) -> p j b", j=TB), ("y^T", f), lambda s: s.rearrange("p (j b) -> p j b", j=TB))
            for e in range(4):
                if e % 2 == 0:
                    copied(("y^T", e))
                copied(("glu", e))
                after(nc.vector.tensor_tensor(tmp[e % 2], tmp[e % 2], yT[:, e, :], ALU.mult))
                nc.vector.tensor_tensor(y_ssm[:, e, :], tmp[e % 2], zs[:, e, :], ALU.mult).then_inc(glu_ready, 1)
            for m in range(KC):
                name = ("out", m)
                nc.vector.tensor_tensor(xT[:, m, :], xT[:, m, :], ready(name), ALU.add).then_inc(free(name), 1)
                sum_squares(6, m - 1)
            norm(6)
            for t in range(1, ST, 2):
                copy(arena[:, S * t:S * t + S], ("store", t))


_INS = ["x", "c", "ada_w", "ada_b", "norm_mix", "norm_ffn", "ffn_w_in", "ffn_w_out", "a_w_in", "a_w_out", "a_sink", "b_w_in", "b_w_out",
        "final_norm", "norm_gain_2", "w_in_2", "ssm_a_re_2", "ssm_a_im_2", "ssm_log_dt_2", "ssm_b_re_2", "ssm_b_im_2", "ssm_c_re_2",
        "ssm_c_im_2", "ssm_d_2", "w_glu_2", "b_glu_2", "conv_w_2", "w_out_2", "final_norm_gain_2"]
_OUTS = [((1, 1024, 1024), "float32")]


def kernel(**inputs):
    import numpy as _np
    import concourse.bacc as _bacc
    from concourse import mybir as _mybir
    from concourse.bass_utils import run_bass_kernel_spmd as _run

    nc = _bacc.Bacc("TRN2", target_bir_lowering=False, num_devices=1)
    arrays, args = {}, []
    for name in _INS:
        a = _np.ascontiguousarray(inputs[name])
        arrays[f"in_{name}_dram"] = a
        args.append(nc.dram_tensor(f"in_{name}_dram", a.shape, _mybir.dt.from_np(a.dtype), kind="ExternalInput").ap())
    for i, (shape, dtype) in enumerate(_OUTS):
        dt = _mybir.dt.from_np(_np.dtype(dtype))
        args.append(nc.dram_tensor(f"out_{i}_dram", shape, dt, kind="ExternalOutput").ap())
    two_blocks_kernel(nc, *args)
    r = _run(nc, [arrays], core_ids=[0])
    return r.results[0]["out_0_dram"]
```
